# Optimizing a Trainium2 kernel written in Bass

```python
import math
import jax, jax.numpy as jnp
from jax import lax
import numpy as np
import jax
import jax.numpy as jnp

D_MODEL = 2048
BATCH = 1
SEQ = 256
DEPTH = 1

SB_HEADS = 8
SB_HEAD_DIM = 128
SB_WIDTH = SB_HEADS * SB_HEAD_DIM
Q_BLOCK = 128
S5_WIDTH = 1024
S5_GROUP = 16
S5_GROUPS = S5_WIDTH // S5_GROUP
S5_STATE = 64
ML_HEADS = 4
ML_HEAD_DIM = 256
ML_WIDTH = ML_HEADS * ML_HEAD_DIM
ML_CHUNK = 64
ML_CONV = 4
N_GROUPS = 4
EXPERTS_PER_GROUP = 8
N_EXPERTS = N_GROUPS * EXPERTS_PER_GROUP
TOP_K = 2
EXPERT_FF = 256
EPS = 1e-6

IN_SIZES = (SB_WIDTH, SB_WIDTH, SB_WIDTH,
            S5_WIDTH,
            ML_WIDTH, ML_WIDTH, ML_WIDTH, ML_WIDTH,
            ML_HEADS, ML_HEADS,
            D_MODEL, D_MODEL, D_MODEL)
IN_COLS = sum(IN_SIZES)


def rms_norm(x, g):
    xf = x.astype(jnp.float32)
    y = xf * lax.rsqrt(jnp.mean(xf * xf, axis=-1, keepdims=True) + EPS)
    return (y * g.astype(jnp.float32)).astype(x.dtype)

def modulate(h, shift, scale):
    return h * (1.0 + scale[:, None, :]) + shift[:, None, :]

def stick_breaking_attention(q, k, v):
    bsz, seq, nh, dh = q.shape
    nb = seq // Q_BLOCK
    qb = q.reshape(bsz, nb, Q_BLOCK, nh, dh).transpose(1, 0, 3, 2, 4)
    kpos = jnp.arange(seq)
    scale = dh ** -0.5

    def block(args):
        qi, bi = args
        qpos = bi * Q_BLOCK + jnp.arange(Q_BLOCK)
        z = jnp.einsum('bhqd,bshd->bhqs', qi, k).astype(jnp.float32) * scale
        causal = kpos[None, :] < qpos[:, None]
        log_beta = jax.nn.log_sigmoid(z)
        log_keep = jnp.where(causal, jax.nn.log_sigmoid(-z), 0.0)
        rest = lax.cumsum(log_keep, axis=3, reverse=True) - log_keep
        w = jnp.where(causal, jnp.exp(log_beta + rest), 0.0)
        return jnp.einsum('bhqs,bshd->bhqd', w.astype(v.dtype), v)

    out = lax.map(block, (qb, jnp.arange(nb)))
    return out.transpose(1, 0, 3, 2, 4).reshape(bsz, seq, nh * dh)

def _linear_recurrence_combine(left, right):
    a_l, b_l = left
    a_r, b_r = right
    return a_r * a_l, a_r * b_l + b_r

def s5_layer(u, lam_re, lam_im, log_dt, b_re, b_im, c_re, c_im, d_skip, w_glu):
    bsz, seq, _ = u.shape
    f32 = jnp.float32
    uf = u.astype(f32).reshape(bsz, seq, S5_GROUPS, S5_GROUP)
    lam = lax.complex(lam_re.astype(f32), lam_im.astype(f32))
    dt = jnp.exp(log_dt.astype(f32))[:, None]
    lam_bar = jnp.exp(lam * dt)
    b_bar = ((lam_bar - 1.0) / lam)[:, :, None] * lax.complex(b_re.astype(f32), b_im.astype(f32))
    bu = jnp.einsum('bsgh,gph->bsgp', uf.astype(jnp.complex64), b_bar)
    a = jnp.broadcast_to(lam_bar, bu.shape)
    _, states = lax.associative_scan(_linear_recurrence_combine, (a, bu), axis=1)
    c_mat = lax.complex(c_re.astype(f32), c_im.astype(f32))
    y = jnp.einsum('bsgp,ghp->bsgh', states, c_mat).real \
        + d_skip.astype(f32).reshape(S5_GROUPS, S5_GROUP) * uf
    y = jax.nn.gelu(y.reshape(bsz, seq, S5_WIDTH))
    y = y * jax.nn.sigmoid(y @ w_glu.astype(f32))
    return y.astype(u.dtype)

def causal_depthwise_conv(x, w):
    width, ch = w.shape
    return lax.conv_general_dilated(x, w[:, None, :].astype(x.dtype), window_strides=(1,),
                                    padding=[(width - 1, 0)],
                                    dimension_numbers=('NWC', 'WIO', 'NWC'),
                                    feature_group_count=ch)

def mlstm_chunkwise(q, k, v, i_pre, f_pre):
    bsz, seq, nh, dh = q.shape
    f32 = jnp.float32
    L = ML_CHUNK
    nc = seq // L
    q = q.astype(f32).reshape(bsz, nc, L, nh, dh)
    k = k.astype(f32).reshape(bsz, nc, L, nh, dh) * (dh ** -0.5)
    v = v.astype(f32).reshape(bsz, nc, L, nh, dh)
    log_i = i_pre.astype(f32).reshape(bsz, nc, L, nh)
    log_f = jax.nn.log_sigmoid(f_pre.astype(f32)).reshape(bsz, nc, L, nh)
    b = jnp.cumsum(log_f, axis=2)
    b_tot = b[:, :, -1]
    a = b_tot[:, :, None] - b + log_i
    m_loc = jnp.max(a, axis=2)
    wa = jnp.exp(a - m_loc[:, :, None])
    d_c = jnp.einsum('bclh,bclhv,bclhk->bchvk', wa, v, k)
    d_n = jnp.einsum('bclh,bclhk->bchk', wa, k)

    def step(carry, inp):
        c_st, n_st, m_st = carry
        dc, dn, ml, bt = inp
        m_new = jnp.maximum(bt + m_st, ml)
        s_old = jnp.exp(bt + m_st - m_new)
        s_new = jnp.exp(ml - m_new)
        c_new = s_old[..., None, None] * c_st + s_new[..., None, None] * dc
        n_new = s_old[..., None] * n_st + s_new[..., None] * dn
        return (c_new, n_new, m_new), (c_st, n_st, m_st)

    init = (jnp.zeros((bsz, nh, dh, dh), f32), jnp.zeros((bsz, nh, dh), f32), jnp.zeros((bsz, nh), f32))
    _, (c0, n0, m0) = lax.scan(step, init, (jnp.moveaxis(d_c, 1, 0), jnp.moveaxis(d_n, 1, 0),
                                             jnp.moveaxis(m_loc, 1, 0), jnp.moveaxis(b_tot, 1, 0)))
    c0 = jnp.moveaxis(c0, 0, 1)
    n0 = jnp.moveaxis(n0, 0, 1)
    m0 = jnp.moveaxis(m0, 0, 1)
    tril = jnp.tril(jnp.ones((L, L), dtype=bool))
    log_d = b[:, :, :, None, :] - b[:, :, None, :, :] + log_i[:, :, None, :, :]
    log_d = jnp.where(tril[None, None, :, :, None], log_d, -jnp.inf)
    inter_log = b + m0[:, :, None, :]
    m_t = jnp.maximum(inter_log, jnp.max(log_d, axis=3))
    d_w = jnp.exp(log_d - m_t[:, :, :, None, :])
    w_inter = jnp.exp(inter_log - m_t)
    s_mat = d_w * jnp.einsum('bclhd,bcshd->bclsh', q, k)
    num = jnp.einsum('bclsh,bcshv->bclhv', s_mat, v) \
        + w_inter[..., None] * jnp.einsum('bchvk,bclhk->bclhv', c0, q)
    den = jnp.sum(s_mat, axis=3) + w_inter * jnp.einsum('bchk,bclhk->bclh', n0, q)
    h = num / jnp.maximum(jnp.abs(den), jnp.exp(-m_t))[..., None]
    return h.reshape(bsz, seq, nh * dh)

def hierarchical_moe(h, w_group, b_group, w_router, b_router, w1, w3, w2):
    bsz, seq, dm = h.shape
    t = h.reshape(-1, dm)
    g_logits = (t @ w_group).astype(jnp.float32) + b_group.astype(jnp.float32)
    g_prob = jax.nn.softmax(g_logits, axis=-1)
    g_idx = jnp.argmax(g_logits, axis=-1)
    g_w = jnp.take_along_axis(g_prob, g_idx[:, None], axis=-1)
    e_logits = ((t @ w_router).astype(jnp.float32) + b_router.astype(jnp.float32)).reshape(-1, N_GROUPS, EXPERTS_PER_GROUP)
    e_in_group = jnp.take_along_axis(e_logits, g_idx[:, None, None], axis=1)[:, 0]
    top_v, top_i = lax.top_k(e_in_group, TOP_K)
    top_w = jax.nn.softmax(top_v, axis=-1) * g_w
    within = jnp.sum(jax.nn.one_hot(top_i, EXPERTS_PER_GROUP, dtype=jnp.float32) * top_w[..., None], axis=1)
    gates = (jax.nn.one_hot(g_idx, N_GROUPS, dtype=jnp.float32)[:, :, None] * within[:, None, :]).reshape(-1, N_EXPERTS)
    hid = jax.nn.silu(jnp.einsum('td,edf->tef', t, w1)) * jnp.einsum('td,edf->tef', t, w3)
    y = jnp.einsum('tef,efd->td', hid * gates.astype(hid.dtype)[:, :, None], w2)
    return y.reshape(bsz, seq, dm)

def first_inputs(seed: int = 0) -> dict:
    key = jax.random.key(seed)
    ks = jax.random.split(key, 40)
    f32 = jnp.float32
    L = DEPTH
    D = D_MODEL

    def nrm(k, shape, scale):
        return jax.random.normal(k, shape, f32) * scale

    n_idx = jnp.arange(S5_STATE, dtype=f32)
    return {
        'x': nrm(ks[0], (BATCH, SEQ, D), 1.0),
        'c': nrm(ks[1], (BATCH, D), 1.0),
        'norm_mix_g': 1.0 + nrm(ks[2], (L, D), 0.02),
        'norm_moe_g': 1.0 + nrm(ks[3], (L, D), 0.02),
        'final_g': 1.0 + nrm(ks[4], (D,), 0.02),
        'w_ada': nrm(ks[5], (L, D, 6 * D), 0.5 * D ** -0.5),
        'b_ada': nrm(ks[6], (L, 6 * D), 0.02),
        'w_in': nrm(ks[7], (L, D, IN_COLS), D ** -0.5),
        'ml_conv': nrm(ks[8], (L, ML_CONV, 2 * ML_WIDTH), 0.5),
        'ml_i_bias': nrm(ks[9], (L, ML_HEADS), 0.1),
        'ml_f_bias': jnp.linspace(3.0, 6.0, ML_HEADS, dtype=f32)[None, :] + nrm(ks[10], (L, ML_HEADS), 0.1),
        's5_lam_re': -0.5 + nrm(ks[11], (L, S5_GROUPS, S5_STATE), 0.01),
        's5_lam_im': math.pi * n_idx[None, None, :] + nrm(ks[12], (L, S5_GROUPS, S5_STATE), 0.01),
        's5_log_dt': jax.random.uniform(ks[13], (L, S5_GROUPS), f32, math.log(1e-3), math.log(1e-1)),
        's5_b_re': nrm(ks[14], (L, S5_GROUPS, S5_STATE, S5_GROUP), (2 * S5_GROUP) ** -0.5),
        's5_b_im': nrm(ks[15], (L, S5_GROUPS, S5_STATE, S5_GROUP), (2 * S5_GROUP) ** -0.5),
        's5_c_re': nrm(ks[16], (L, S5_GROUPS, S5_GROUP, S5_STATE), S5_STATE ** -0.5),
        's5_c_im': nrm(ks[17], (L, S5_GROUPS, S5_GROUP, S5_STATE), S5_STATE ** -0.5),
        's5_d': nrm(ks[18], (L, S5_WIDTH), 0.5),
        's5_w_glu': nrm(ks[19], (L, S5_WIDTH, S5_WIDTH), S5_WIDTH ** -0.5),
        'p_sb': nrm(ks[20], (L, SB_WIDTH, D), SB_WIDTH ** -0.5),
        'p_s5': nrm(ks[21], (L, S5_WIDTH, D), S5_WIDTH ** -0.5),
        'p_ml': nrm(ks[22], (L, ML_WIDTH, D), ML_WIDTH ** -0.5),
        'w_out': nrm(ks[23], (L, D, D), D ** -0.5),
        'moe_w_group': nrm(ks[24], (L, D, N_GROUPS), D ** -0.5),
        'moe_b_group': nrm(ks[25], (L, N_GROUPS), 0.01),
        'moe_w_router': nrm(ks[26], (L, D, N_EXPERTS), D ** -0.5),
        'moe_b_router': nrm(ks[27], (L, N_EXPERTS), 0.01),
        'moe_w1': nrm(ks[28], (L, N_EXPERTS, D, EXPERT_FF), D ** -0.5),
        'moe_w3': nrm(ks[29], (L, N_EXPERTS, D, EXPERT_FF), D ** -0.5),
        'moe_w2': nrm(ks[30], (L, N_EXPERTS, EXPERT_FF, D), EXPERT_FF ** -0.5),
    }

def first_block(x, c, norm_mix_g, norm_moe_g, final_g, w_ada, b_ada, w_in, ml_conv, ml_i_bias, ml_f_bias,
              s5_lam_re, s5_lam_im, s5_log_dt, s5_b_re, s5_b_im, s5_c_re, s5_c_im, s5_d, s5_w_glu,
              p_sb, p_s5, p_ml, w_out, moe_w_group, moe_b_group, moe_w_router, moe_b_router,
              moe_w1, moe_w3, moe_w2):
    bsz, seq, _ = x.shape
    split_points = [int(p) for p in np.cumsum(IN_SIZES)[:-1]]
    c_act = jax.nn.silu(c)
    for l in range(DEPTH):
        mod = c_act @ w_ada[l] + b_ada[l]
        shift1, scale1, gate1, shift2, scale2, gate2 = jnp.split(mod, 6, axis=-1)

        h = modulate(rms_norm(x, norm_mix_g[l]), shift1, scale1)
        proj = h @ w_in[l]
        (sb_q, sb_k, sb_v, s5_u, ml_q, ml_k, ml_v, ml_o, ml_i, ml_f,
         g_sb, g_s5, g_ml) = jnp.split(proj, split_points, axis=-1)

        sb_shape = (bsz, seq, SB_HEADS, SB_HEAD_DIM)
        y_sb = stick_breaking_attention(sb_q.reshape(sb_shape), sb_k.reshape(sb_shape), sb_v.reshape(sb_shape))

        y_s5 = s5_layer(s5_u, s5_lam_re[l], s5_lam_im[l], s5_log_dt[l], s5_b_re[l], s5_b_im[l],
                        s5_c_re[l], s5_c_im[l], s5_d[l], s5_w_glu[l])

        qk = jax.nn.silu(causal_depthwise_conv(jnp.concatenate([ml_q, ml_k], axis=-1), ml_conv[l]))
        ml_q_c, ml_k_c = jnp.split(qk, 2, axis=-1)
        ml_shape = (bsz, seq, ML_HEADS, ML_HEAD_DIM)
        y_ml = mlstm_chunkwise(ml_q_c.reshape(ml_shape), ml_k_c.reshape(ml_shape), ml_v.reshape(ml_shape),
                               ml_i + ml_i_bias[l], ml_f + ml_f_bias[l])
        y_ml = (y_ml * jax.nn.sigmoid(ml_o.astype(jnp.float32))).astype(x.dtype)

        merged = jax.nn.sigmoid(g_sb) * (y_sb @ p_sb[l]) \
            + jax.nn.sigmoid(g_s5) * (y_s5 @ p_s5[l]) \
            + jax.nn.sigmoid(g_ml) * (y_ml @ p_ml[l])
        x = x + gate1[:, None, :] * (merged @ w_out[l])

        h = modulate(rms_norm(x, norm_moe_g[l]), shift2, scale2)
        x = x + gate2[:, None, :] * hierarchical_moe(h, moe_w_group[l], moe_b_group[l], moe_w_router[l],
                                                     moe_b_router[l], moe_w1[l], moe_w3[l], moe_w2[l])
    return rms_norm(x, final_g)


HEAD_DIM = 128
BRANCH_WIDTH = D_MODEL // 2
N_BRANCH = 3
PLE_DIM = 256
NORM_EPS = 1e-6

LRU_BLOCK = 64
LRU_BLOCKS = BRANCH_WIDTH // LRU_BLOCK
CONV_WIDTH = 4
LRU_C = 8.0

NSA_HEADS = BRANCH_WIDTH // HEAD_DIM
NSA_KV_HEADS = 2
NSA_GROUP = NSA_HEADS // NSA_KV_HEADS
NSA_KV_WIDTH = NSA_KV_HEADS * HEAD_DIM
CMP_BLOCK = 32
CMP_STRIDE = 16
CMP_HIDDEN = 256
SEL_BLOCK = 64
SEL_TOPK = 16
WINDOW = 512
NSA_Q_BLOCK = 32

FOX_HEADS = BRANCH_WIDTH // HEAD_DIM
FOX_Q_BLOCK = 128
FORGET_BIAS = 3.0

IN_SPLITS = (
    ('lru_x', BRANCH_WIDTH), ('lru_gate', BRANCH_WIDTH),
    ('nsa_q', BRANCH_WIDTH),
    ('nsa_k_cmp', NSA_KV_WIDTH), ('nsa_v_cmp', NSA_KV_WIDTH),
    ('nsa_k_slc', NSA_KV_WIDTH), ('nsa_v_slc', NSA_KV_WIDTH),
    ('nsa_k_win', NSA_KV_WIDTH), ('nsa_v_win', NSA_KV_WIDTH),
    ('nsa_bgate', NSA_HEADS * 3), ('nsa_gate', BRANCH_WIDTH),
    ('fox_q', BRANCH_WIDTH), ('fox_k', BRANCH_WIDTH), ('fox_v', BRANCH_WIDTH),
    ('fox_f', FOX_HEADS), ('fox_gate', BRANCH_WIDTH),
    ('merge', N_BRANCH * D_MODEL),
)
N_IN = sum(size for _, size in IN_SPLITS)


def column_offsets():
    offs, start = {}, 0
    for name, size in IN_SPLITS:
        offs[name] = (start, size)
        start += size
    return offs

def split_columns(z):
    return {name: z[..., s:s + n] for name, (s, n) in column_offsets().items()}

def split_heads(t, n_heads):
    b, s, _ = t.shape
    return t.reshape(b, s, n_heads, HEAD_DIM)

def rms_norm_2(x, gain):
    xf = x.astype(jnp.float32)
    y = xf * lax.rsqrt(jnp.mean(xf * xf, axis=-1, keepdims=True) + NORM_EPS)
    return (y * gain.astype(jnp.float32)).astype(x.dtype)

def masked_softmax(logits, mask):
    logits = jnp.where(mask, logits.astype(jnp.float32), -jnp.inf)
    m = jnp.max(logits, axis=-1, keepdims=True)
    m = jnp.where(jnp.isfinite(m), m, 0.0)
    e = jnp.exp(logits - m)
    return e / jnp.maximum(jnp.sum(e, axis=-1, keepdims=True), 1e-30)

def linear_combine(left, right):
    a_l, b_l = left
    a_r, b_r = right
    return a_l * a_r, a_r * b_l + b_r

def rglru_branch(u, conv_w, conv_b, wa, ba, wx, bx, lam):
    b, s, w = u.shape
    taps = conv_w[:, None, :].astype(u.dtype)
    uc = lax.conv_general_dilated(u, taps, (1,), ((CONV_WIDTH - 1, 0),),
                                  dimension_numbers=('NWC', 'WIO', 'NWC'),
                                  feature_group_count=w) + conv_b
    ub = uc.reshape(b, s, LRU_BLOCKS, LRU_BLOCK)
    rec = jax.nn.sigmoid((jnp.einsum('bsnk,nkj->bsnj', ub, wa).reshape(b, s, w) + ba).astype(jnp.float32))
    inp = jax.nn.sigmoid((jnp.einsum('bsnk,nkj->bsnj', ub, wx).reshape(b, s, w) + bx).astype(jnp.float32))
    log_a = -LRU_C * rec * jax.nn.softplus(-lam.astype(jnp.float32))
    a = jnp.exp(log_a)
    drive = jnp.sqrt(-jnp.expm1(2.0 * log_a)) * (inp * uc.astype(jnp.float32))
    _, hseq = lax.associative_scan(linear_combine, (a, drive), axis=1)
    return hseq.astype(u.dtype)

def compress(t, pos, w1, w2):
    b, s, hk, dk = t.shape
    n_chunk = s // CMP_STRIDE
    ratio = CMP_BLOCK // CMP_STRIDE
    n_cmp = n_chunk - ratio + 1
    chunks = t.reshape(b, n_chunk, CMP_STRIDE, hk, dk)
    blocks = jnp.concatenate([chunks[:, r:r + n_cmp] for r in range(ratio)], axis=2)
    blocks = blocks + pos[:, None, :]
    flat = blocks.transpose(0, 1, 3, 2, 4).reshape(b, n_cmp, hk, CMP_BLOCK * dk)
    return jax.nn.silu(flat @ w1) @ w2

def nsa_branch(q, kc, vc, ks, vs, kw, vw, gates):
    b, s, h, dk = q.shape
    scale = dk ** -0.5
    n_cmp = kc.shape[1]
    n_sel = s // SEL_BLOCK
    n_top = min(SEL_TOPK, n_sel)
    nb = s // NSA_Q_BLOCK
    cmp_start = jnp.arange(n_cmp) * CMP_STRIDE
    cmp_end = cmp_start + CMP_BLOCK - 1
    sel_ids = jnp.arange(n_sel)
    sel_start = sel_ids * SEL_BLOCK
    overlap = ((cmp_start[:, None] < sel_start[None, :] + SEL_BLOCK)
               & (cmp_start[:, None] + CMP_BLOCK > sel_start[None, :])).astype(jnp.float32)
    ks_blk = ks.reshape(b, n_sel, SEL_BLOCK, NSA_KV_HEADS, dk).transpose(0, 3, 1, 2, 4)
    vs_blk = vs.reshape(b, n_sel, SEL_BLOCK, NSA_KV_HEADS, dk).transpose(0, 3, 1, 2, 4)
    bi = jnp.arange(b)[:, None, None, None]
    gi = jnp.arange(NSA_KV_HEADS)[None, None, :, None]
    pad = ((0, 0), (WINDOW, 0), (0, 0), (0, 0))
    kw_pad = jnp.pad(kw, pad)
    vw_pad = jnp.pad(vw, pad)
    win_off = jnp.arange(WINDOW + NSA_Q_BLOCK) - WINDOW
    q_blocks = q.reshape(b, nb, NSA_Q_BLOCK, NSA_KV_HEADS, NSA_GROUP, dk).swapaxes(0, 1)
    g_blocks = gates.reshape(b, nb, NSA_Q_BLOCK, NSA_KV_HEADS, NSA_GROUP, 3).swapaxes(0, 1)
    t0s = jnp.arange(nb, dtype=jnp.int32) * NSA_Q_BLOCK
    flat_sel = n_top * SEL_BLOCK

    def block(args):
        qb, gb, t0 = args
        tq = t0 + jnp.arange(NSA_Q_BLOCK)
        s_c = jnp.einsum('btgqd,bcgd->btgqc', qb, kc) * scale
        m_c = (cmp_end[None, :] <= tq[:, None])[None, :, None, None, :]
        p_c = masked_softmax(s_c, m_c)
        o_c = jnp.einsum('btgqc,bcgd->btgqd', p_c.astype(vc.dtype), vc)
        imp = jnp.einsum('btgqc,cj->btgj', p_c, overlap)
        cur = (tq // SEL_BLOCK)[:, None]
        valid = sel_ids[None, :] <= cur
        forced = (sel_ids[None, :] == 0) | (sel_ids[None, :] == cur) | (sel_ids[None, :] == cur - 1)
        score = jnp.where(forced[None, :, None, :], jnp.inf,
                          jnp.where(valid[None, :, None, :], imp, -jnp.inf))
        _, idx = lax.top_k(score, n_top)
        k_sel = ks_blk[bi, gi, idx]
        v_sel = vs_blk[bi, gi, idx]
        s_s = jnp.einsum('btgqd,btgnkd->btgqnk', qb, k_sel) * scale
        kpos = idx[..., None] * SEL_BLOCK + jnp.arange(SEL_BLOCK)
        m_s = kpos <= tq[None, :, None, None, None]
        p_s = masked_softmax(s_s.reshape(b, NSA_Q_BLOCK, NSA_KV_HEADS, NSA_GROUP, flat_sel),
                             m_s.reshape(b, NSA_Q_BLOCK, NSA_KV_HEADS, 1, flat_sel))
        o_s = jnp.einsum('btgqm,btgmd->btgqd', p_s.astype(vs.dtype),
                         v_sel.reshape(b, NSA_Q_BLOCK, NSA_KV_HEADS, flat_sel, dk))
        k_w = lax.dynamic_slice_in_dim(kw_pad, t0, WINDOW + NSA_Q_BLOCK, axis=1)
        v_w = lax.dynamic_slice_in_dim(vw_pad, t0, WINDOW + NSA_Q_BLOCK, axis=1)
        wpos = t0 + win_off
        m_w = ((wpos[None, :] >= 0) & (wpos[None, :] <= tq[:, None])
               & (wpos[None, :] > tq[:, None] - WINDOW))[None, :, None, None, :]
        s_w = jnp.einsum('btgqd,bkgd->btgqk', qb, k_w) * scale
        p_w = masked_softmax(s_w, m_w)
        o_w = jnp.einsum('btgqk,bkgd->btgqd', p_w.astype(vw.dtype), v_w)
        return gb[..., 0:1] * o_c + gb[..., 1:2] * o_s + gb[..., 2:3] * o_w

    out = lax.map(block, (q_blocks, g_blocks, t0s))
    return out.swapaxes(0, 1).reshape(b, s, h * dk)

def fox_branch(q, k, v, log_f):
    b, s, h, dk = q.shape
    scale = dk ** -0.5
    nb = s // FOX_Q_BLOCK
    c = jnp.cumsum(log_f, axis=1)
    ck = c.transpose(0, 2, 1)
    kpos = jnp.arange(s)
    q_blocks = q.reshape(b, nb, FOX_Q_BLOCK, h, dk).swapaxes(0, 1)
    c_blocks = c.reshape(b, nb, FOX_Q_BLOCK, h).swapaxes(0, 1)
    t0s = jnp.arange(nb, dtype=jnp.int32) * FOX_Q_BLOCK

    def block(args):
        qb, cb, t0 = args
        tq = t0 + jnp.arange(FOX_Q_BLOCK)
        logits = jnp.einsum('bqhd,bkhd->bhqk', qb, k).astype(jnp.float32) * scale
        logits = logits + (cb.transpose(0, 2, 1)[..., None] - ck[:, :, None, :])
        p_att = masked_softmax(logits, kpos[None, :] <= tq[:, None])
        return jnp.einsum('bhqk,bkhd->bqhd', p_att.astype(v.dtype), v)

    out = lax.map(block, (q_blocks, c_blocks, t0s))
    return out.swapaxes(0, 1).reshape(b, s, h * dk)

def second_inputs(seed: int = 0) -> dict:
    key = jax.random.key(seed)
    ks = jax.random.split(key, 26)
    f32 = jnp.float32

    def nrm(k, shape, fan_in):
        return jax.random.normal(k, shape, f32) * (fan_in ** -0.5)

    def gain(k, shape):
        return 1.0 + 0.05 * jax.random.normal(k, shape, f32)

    def small(k, shape):
        return 0.02 * jax.random.normal(k, shape, f32)

    x = jax.random.normal(ks[0], (BATCH, SEQ, D_MODEL), f32)
    p = jax.random.normal(ks[1], (DEPTH, BATCH, SEQ, PLE_DIM), f32)
    ln_gain = gain(ks[2], (DEPTH, D_MODEL))
    w_in = nrm(ks[3], (DEPTH, D_MODEL, N_IN), D_MODEL)
    f_off = column_offsets()['fox_f'][0]
    b_in = small(ks[4], (DEPTH, N_IN)).at[:, f_off:f_off + FOX_HEADS].add(FORGET_BIAS)
    conv_w = nrm(ks[5], (DEPTH, CONV_WIDTH, BRANCH_WIDTH), CONV_WIDTH)
    conv_b = small(ks[6], (DEPTH, BRANCH_WIDTH))
    lru_wa = nrm(ks[7], (DEPTH, LRU_BLOCKS, LRU_BLOCK, LRU_BLOCK), LRU_BLOCK)
    lru_ba = small(ks[8], (DEPTH, BRANCH_WIDTH))
    lru_wx = nrm(ks[9], (DEPTH, LRU_BLOCKS, LRU_BLOCK, LRU_BLOCK), LRU_BLOCK)
    lru_bx = small(ks[10], (DEPTH, BRANCH_WIDTH))
    a0 = jax.random.uniform(ks[11], (DEPTH, BRANCH_WIDTH), f32, minval=0.9, maxval=0.999)
    root = a0 ** (1.0 / LRU_C)
    lru_lambda = jnp.log(root) - jnp.log1p(-root)
    cmp_w1 = nrm(ks[12], (DEPTH, 2, CMP_BLOCK * HEAD_DIM, CMP_HIDDEN), CMP_BLOCK * HEAD_DIM)
    cmp_w2 = nrm(ks[13], (DEPTH, 2, CMP_HIDDEN, HEAD_DIM), CMP_HIDDEN)
    cmp_pos = small(ks[14], (DEPTH, 2, CMP_BLOCK, HEAD_DIM))
    nsa_q_gain = gain(ks[15], (DEPTH, HEAD_DIM))
    nsa_k_gain = gain(ks[16], (DEPTH, HEAD_DIM))
    fox_q_gain = gain(ks[17], (DEPTH, HEAD_DIM))
    fox_k_gain = gain(ks[18], (DEPTH, HEAD_DIM))
    w_branch = nrm(ks[19], (DEPTH, N_BRANCH, BRANCH_WIDTH, D_MODEL), BRANCH_WIDTH)
    w_out = nrm(ks[20], (DEPTH, D_MODEL, D_MODEL), D_MODEL)
    w_ple = nrm(ks[21], (DEPTH, PLE_DIM, D_MODEL), PLE_DIM)
    ple_gain = gain(ks[22], (DEPTH, D_MODEL))
    w_ple_gate = nrm(ks[23], (DEPTH, D_MODEL, D_MODEL), D_MODEL)
    return {'x': x, 'p': p, 'ln_gain': ln_gain, 'w_in': w_in, 'b_in': b_in,
            'conv_w': conv_w, 'conv_b': conv_b, 'lru_wa': lru_wa, 'lru_ba': lru_ba,
            'lru_wx': lru_wx, 'lru_bx': lru_bx, 'lru_lambda': lru_lambda,
            'cmp_w1': cmp_w1, 'cmp_w2': cmp_w2, 'cmp_pos': cmp_pos,
            'nsa_q_gain': nsa_q_gain, 'nsa_k_gain': nsa_k_gain,
            'fox_q_gain': fox_q_gain, 'fox_k_gain': fox_k_gain,
            'w_branch': w_branch, 'w_out': w_out, 'w_ple': w_ple,
            'ple_gain': ple_gain, 'w_ple_gate': w_ple_gate}

def second_block(x, p, ln_gain, w_in, b_in, conv_w, conv_b, lru_wa, lru_ba, lru_wx, lru_bx,
              lru_lambda, cmp_w1, cmp_w2, cmp_pos, nsa_q_gain, nsa_k_gain, fox_q_gain,
              fox_k_gain, w_branch, w_out, w_ple, ple_gain, w_ple_gate):
    b, s, _ = x.shape
    h = x
    for l in range(DEPTH):
        hn = rms_norm_2(h, ln_gain[l])
        z = split_columns(hn @ w_in[l] + b_in[l])
        y_a = rglru_branch(z['lru_x'], conv_w[l], conv_b[l], lru_wa[l], lru_ba[l],
                           lru_wx[l], lru_bx[l], lru_lambda[l]) * jax.nn.silu(z['lru_gate'])
        q_b = rms_norm_2(split_heads(z['nsa_q'], NSA_HEADS), nsa_q_gain[l])
        k_c = rms_norm_2(compress(split_heads(z['nsa_k_cmp'], NSA_KV_HEADS), cmp_pos[l, 0],
                                cmp_w1[l, 0], cmp_w2[l, 0]), nsa_k_gain[l])
        v_c = compress(split_heads(z['nsa_v_cmp'], NSA_KV_HEADS), cmp_pos[l, 1],
                       cmp_w1[l, 1], cmp_w2[l, 1])
        k_s = rms_norm_2(split_heads(z['nsa_k_slc'], NSA_KV_HEADS), nsa_k_gain[l])
        v_s = split_heads(z['nsa_v_slc'], NSA_KV_HEADS)
        k_w = rms_norm_2(split_heads(z['nsa_k_win'], NSA_KV_HEADS), nsa_k_gain[l])
        v_w = split_heads(z['nsa_v_win'], NSA_KV_HEADS)
        g_b = jax.nn.sigmoid(z['nsa_bgate']).reshape(b, s, NSA_HEADS, 3)
        y_b = nsa_branch(q_b, k_c, v_c, k_s, v_s, k_w, v_w, g_b) * jax.nn.silu(z['nsa_gate'])
        log_f = jax.nn.log_sigmoid(z['fox_f'].astype(jnp.float32))
        y_c = fox_branch(rms_norm_2(split_heads(z['fox_q'], FOX_HEADS), fox_q_gain[l]),
                         rms_norm_2(split_heads(z['fox_k'], FOX_HEADS), fox_k_gain[l]),
                         split_heads(z['fox_v'], FOX_HEADS), log_f) * jax.nn.silu(z['fox_gate'])
        mg = jax.nn.sigmoid(z['merge']).reshape(b, s, N_BRANCH, D_MODEL)
        merged = (mg[:, :, 0] * (y_a @ w_branch[l, 0])
                  + mg[:, :, 1] * (y_b @ w_branch[l, 1])
                  + mg[:, :, 2] * (y_c @ w_branch[l, 2]))
        h = h + merged @ w_out[l]
        e = rms_norm_2(p[l] @ w_ple[l], ple_gain[l])
        h = h + jax.nn.sigmoid(h @ w_ple_gate[l]) * e
    return h


def setup_inputs(seed=0):
    out = dict(first_inputs(seed))
    for name, value in second_inputs(seed + 1).items():
        if name != "x":
            out[name + "_2"] = value
    return out


def reference(
    x, c, norm_mix_g, norm_moe_g, final_g, w_ada, b_ada, w_in, ml_conv, ml_i_bias, ml_f_bias,
    s5_lam_re, s5_lam_im, s5_log_dt, s5_b_re, s5_b_im, s5_c_re, s5_c_im, s5_d, s5_w_glu, p_sb,
    p_s5, p_ml, w_out, moe_w_group, moe_b_group, moe_w_router, moe_b_router, moe_w1, moe_w3,
    moe_w2, p_2, ln_gain_2, w_in_2, b_in_2, conv_w_2, conv_b_2, lru_wa_2, lru_ba_2, lru_wx_2,
    lru_bx_2, lru_lambda_2, cmp_w1_2, cmp_w2_2, cmp_pos_2, nsa_q_gain_2, nsa_k_gain_2,
    fox_q_gain_2, fox_k_gain_2, w_branch_2, w_out_2, w_ple_2, ple_gain_2, w_ple_gate_2,
):
    x = first_block(
        x, c, norm_mix_g, norm_moe_g, final_g, w_ada, b_ada, w_in, ml_conv, ml_i_bias,
        ml_f_bias, s5_lam_re, s5_lam_im, s5_log_dt, s5_b_re, s5_b_im, s5_c_re, s5_c_im, s5_d,
        s5_w_glu, p_sb, p_s5, p_ml, w_out, moe_w_group, moe_b_group, moe_w_router, moe_b_router,
        moe_w1, moe_w3, moe_w2,
    )
    return second_block(
        x, p_2, ln_gain_2, w_in_2, b_in_2, conv_w_2, conv_b_2, lru_wa_2, lru_ba_2, lru_wx_2,
        lru_bx_2, lru_lambda_2, cmp_w1_2, cmp_w2_2, cmp_pos_2, nsa_q_gain_2, nsa_k_gain_2,
        fox_q_gain_2, fox_k_gain_2, w_branch_2, w_out_2, w_ple_2, ple_gain_2, w_ple_gate_2,
    )


_drawn_inputs = setup_inputs


def setup_inputs(seed=0):
    import zlib

    import numpy as np

    out = dict(_drawn_inputs(seed))
    spreads = {}
    factors = {'norm_mix_g': 8.0,
     'norm_moe_g': 5.444,
     'final_g': 3.04,
     'b_ada': 2.825,
     'ml_conv': 4.292,
     'ml_i_bias': 47.757,
     'ml_f_bias': 3.688,
     's5_lam_re': 64.0,
     's5_lam_im': 63.056,
     's5_log_dt': 64.0,
     's5_b_re': 64.0,
     's5_b_im': 64.0,
     's5_c_re': 64.0,
     's5_c_im': 64.0,
     's5_w_glu': 6.478,
     'moe_b_group': 8.0,
     'moe_b_router': 6.919,
     'ln_gain_2': 3.398,
     'conv_b_2': 2.718,
     'lru_ba_2': 42.013,
     'lru_bx_2': 32.702,
     'cmp_pos_2': 8.0,
     'nsa_q_gain_2': 8.0,
     'nsa_k_gain_2': 8.0,
     'fox_q_gain_2': 8.0,
     'fox_k_gain_2': 8.0,
     'ple_gain_2': 8.0}
    for name, (base, spread) in spreads.items():
        noise = np.random.default_rng([zlib.crc32(name.encode()), seed]).standard_normal(out[name].shape)
        drawn = base * np.exp(spread * noise) if base else spread * noise
        out[name] = jnp.asarray(drawn.astype(out[name].dtype))
    for name, factor in factors.items():
        out[name] = (out[name] * factor).astype(out[name].dtype)
    return out
```

```python
import concourse.bass as bass
from concourse import mybir

F32 = mybir.dt.float32
F32R = mybir.dt.float32r
ALU = mybir.AluOpType
ACT = mybir.ActivationFunctionType
AX = mybir.AxisListType.X
ds = bass.ds

P = 128
T = 256
D = 2048
DT = D // P
W = 1024
WT = W // P
CH = 16 * P
EPS = 1e-6
MAGIC = 1.5 * 2.0 ** 23
NEG = -1e30
TWO_PI = 6.283184
SB_SCALE = 128 ** -0.5
ML_SCALE = 256 ** -0.5
N_EXP, N_GRP, PER_GRP = 32, 4, 8
ROUNDS = 4
N_CMP, CMP_PAD = 15, 16

PHASES = [("sb", 32), ("p_sb", 8), ("g_sb", 32), ("glu", 4), ("p_s5", 8), ("g_s5", 32), ("mlif", 1),
          ("ml", 32), ("p_ml", 8), ("g_ml", 32), ("wout", 16), ("router", 1), ("moe", ROUNDS * 48),
          ("kv", 12), ("bf", 1), ("cmp", 8), ("nsa", 32), ("p_a", 8), ("g_a", 16), ("p_b", 8), ("g_b", 16),
          ("fox", 32), ("p_c", 8), ("g_c", 16), ("wout2", 16), ("ple", 2), ("pgate", 16)]
BASE, NMAIN = {}, 0
for _name, _n in PHASES:
    BASE[_name] = NMAIN
    NMAIN += _n
NADA = 48
B2 = {"kv": 0, "bf": 12, "nsa": 13, "g_a": 45, "g_b": 61, "fox": 77, "g_c": 109}
NB2 = 125

VECS = [("b_ada", 96), ("g_mix", 16), ("g_moe", 16), ("g_fin", 16), ("g_ln2", 16), ("g_ple", 16), ("b2", NB2),
        ("conv2", 8 * 4), ("conv2b", 8), ("lru_ba", 8), ("lru_bx", 8), ("lru_lam", 8), ("conv", 4 * 16),
        ("s5_d", 8), ("b_if", 1), ("b_rt", 1), ("nsa_q", 1), ("nsa_k", 1), ("fox_q", 1), ("fox_k", 1),
        ("quarter", 1), ("one", 1), ("c", 16), ("lam_re", 32), ("lam_im", 32), ("log_dt", 32)]
VC, NV = {}, 0
for _name, _n in VECS:
    VC[_name] = NV
    NV += _n


def slot(a, i=0, per=1):
    return a % 4, a // 4 + i * per


def build(nc, dr):
    B0 = 16512
    top = [B0]

    def sb(name, shape, dt=F32, at=None):
        size = 4
        for s in shape[1:]:
            size *= s
        size = (size + 31) // 32 * 32
        if at is None:
            at = top[0]
            top[0] += size
        return nc.alloc_sbuf_tensor_at(name, shape, dt, offset=at)

    stage = sb("stage", [P, 4, CH])
    w_hi = sb("w_hi", [P, 4, CH], F32R)
    w_lo = sb("w_lo", [P, 2, CH], F32R)
    x = sb("x", [P, DT, T])
    xh = sb("xh", [P, DT, T], F32R)
    xl = sb("xl", [P, DT, T], F32R)
    ident = sb("ident", [P, P])
    ones = sb("ones", [P, P])
    vec = sb("vec", [P, NV])
    mod = sb("mod", [P, 96])
    a1 = sb("a1", [P, 16])
    a2 = sb("a2", [P, 16])
    cact = sb("cact", [P, 16])
    no_lo = sb("no_lo", [P, 8], F32R)
    vtmp = sb("vtmp", [P, 56])
    rinv = sb("rinv", [P, T])
    foxf = sb("foxf", [P, T])
    rms_red = sb("rms_red", [P, T])
    D0 = top[0]
    M0 = D0 + 32768
    S0 = M0 + 16384
    END = nc.sbuf_usable_end

    class Area:

        def __init__(self, at, end):
            self.at, self.end = at, end

        def __call__(self, name, shape, dt=F32):
            size = 4
            for s in shape[1:]:
                size *= s
            b = sb(name, shape, dt, at=self.at)
            self.at += (size + 31) // 32 * 32
            assert self.at <= self.end, (name, self.at, self.end)
            return b

    yh = sb("yh", [P, WT, T], F32R, at=D0)
    yl = sb("yl", [P, WT, T], F32R, at=D0 + 8192)
    yh2 = sb("yh2", [P, WT, T], F32R, at=D0 + 16384)
    yl2 = sb("yl2", [P, WT, T], F32R, at=D0 + 24576)
    dh = sb("dh", [P, DT, T], F32R, at=D0)
    dl = sb("dl", [P, DT, T], F32R, at=D0 + 16384)
    sq = sb("sq", [P, DT, T], at=D0)
    ada_acc = sb("ada_acc", [P, 2, CH], at=D0)
    sq1 = sb("sq1", [P, DT, T], at=M0)
    hb = sb("hb", [P, DT, T], at=D0 + 16384)
    merged = sb("merged", [P, DT, T], at=M0)
    ptmp1 = sb("ptmp1", [P, DT, T], at=D0 + 16384)
    ptmp2 = sb("ptmp2", [P, DT, T], at=S0)

    ar = Area(D0 + 16384, M0)
    A = {}
    for n, s in [("q", [P, T]), ("k", [P, T]), ("v", [P, T]), ("u", [P, T]), ("soft", [P, 2, T]),
                 ("zm", [P, 2, T]), ("sp", [P, 2, T]), ("w", [P, 2, T]), ("vtok", [P, 2, P]), ("du", [P, T]),
                 ("bcur", [P, 2, P]), ("tri", [P, P])]:
        A[n] = ar("A_" + n, s)
    ar = Area(M0, S0)
    for n, s in [("ph", [P, 4, T]), ("sin", [P, 4, T]), ("cos", [P, 4, T]), ("t1", [P, 2, T]), ("t2", [P, 2, T])]:
        A[n] = ar("A_" + n, s)
    ar = Area(S0, END)
    for n, s in [("y5", [P, WT, T]), ("vr", [P, 2, T]), ("sc", [P, 2, T]), ("srot", [P, 2, 2, T]),
                 ("craw", [P, 4, 2, 32]), ("cm", [P, 4, 2, 32]), ("c1", [P, 4, 2, 32]), ("c2", [P, 4, 2, 32]),
                 ("mask", [P, 2, T]), ("iota", [P, T]), ("s5p", [P, 14, 32])]:
        A[n] = ar("A_" + n, s)
    ar = Area(S0 + 8192, S0 + 8192 + 6144)
    for n, s in [("y5sg", [P, 2, 2 * T]), ("sg", [P, 2, T])]:
        A[n] = ar("A_" + n, s)
    ar = Area(D0 + 16384, M0)
    B = {}
    for n, s in [("raw", [P, 4, T + 4]), ("cv", [P, 4, T]), ("v", [P, 2, T]), ("so", [P, 2, T]), ("vtok", [P, 2, T])]:
        B[n] = ar("B_" + n, s)
    ar = Area(S0, END)
    for n, s in [("qk", [P, 4, T]), ("dm", [P, 2, T]), ("st", [P, 2, T]), ("stm", [P, 2, T]), ("emt", [P, T]), ("ad", [P, T]),
                 ("rec", [P, T]), ("y", [P, 2, T]), ("rm", [P, 2, T]), ("rows", [P, 2, T]), ("mask", [P, 2, T]),
                 ("gcol", [P, 8]), ("sg", [P, 2, T])]:
        B[n] = ar("B_" + n, s)
    ar = Area(D0 + 16384, M0)
    for n in ["li", "lf", "e", "l", "b", "g", "m", "t"]:
        B[n] = ar("B_r" + n, [P, T])
    side_acc = [sb("side_acc0", [P, CH], at=S0 + 14336), sb("side_acc1", [P, CH], at=S0)]
    ar = Area(S0, END)
    R = {}
    for n, s in [("lg", [64, T]), ("L", [P, 2, 64]), ("gmax", [P, 2]), ("eg", [P, 2, 4]), ("gsum", [P, 2]),
                 ("ginv", [P, 2]), ("g4a", [P, 2, 4, 4]), ("g4b", [P, 2, 4, 4]), ("oh", [P, 2, 4]),
                 ("ep", [P, 2, 4, 8]), ("es", [P, 2, 8]), ("e8a", [P, 2, 8, 8]), ("e8b", [P, 2, 8, 8]),
                 ("sel", [P, 2, 8]), ("emax", [P, 2]), ("ex", [P, 2, 8]), ("esum", [P, 2]), ("einv", [P, 2]),
                 ("wi", [P, 2, 8]), ("gates", [P, 2, 4, 8]), ("gT", [32, T]), ("rm", [32, T]), ("tri", [P, 80]),
                 ("sa", [P, 2, T]), ("sb", [P, 2, T]), ("hid", [P, T]), ("ot", [P, 2, T])]:
        R[n] = ar("R_" + n, s)
    ar = Area(D0, M0)
    C = {}
    for n, s, dt in [("kvraw", [P, 12, T], F32), ("kvsq", [P, 4, T], F32), ("xr", [P, 32, 32], F32),
                     ("xrh", [P, 32, 32], F32R), ("xrl", [P, 32, 32], F32R), ("hidc", [P, 4, 32], F32), ("cw2", [P, 4, P], F32),
                     ("pos", [P, 2, 32], F32), ("bf", [P, T], F32)]:
        C[n] = ar("C_" + n, s, dt)
    for i, at in enumerate((S0, S0 + 4096)):
        C[("vrh", "vrl")[i]] = sb("C_" + ("vrh", "vrl")[i], [P, 32, 32], F32R, at=at)
    hid_rows = sb("hid_rows", [32, 2, T], at=S0 + 16384)
    ar = Area(M0, S0)
    for n, s in [("ks", [P, 4, T]), ("vtok", [P, 4, 2, P]), ("q", [P, T]), ("qn", [P, T]), ("ng", [P, 2, T]), ("lg", [P, 2, T]),
                 ("qs", [P, T]), ("rq", [P, T])]:
        C[n] = ar("C_" + n, s)
    ar = Area(S0, END)
    for n, s in [("z", [P, 4, T]), ("pT", [P, 2, 384]), ("pcT", [16, T]), ("mask", [P, 2, T]), ("mcmp", [P, 2, 16]), ("zc", [P, 2, 16]),
                 ("mx", [P, 8]), ("sm", [P, 8]), ("gt", [P, 2, 24]), ("kcn", [P, 2, 16]), ("vct", [16, 2, P]),
                 
                 ("wab", [P, 2, P]), ("raw", [P, T + 4]), ("uc", [P, T]), ("ri", [P, 2, T]), ("th", [P, T]), ("sqv", [P, T]),
                 ("rcp", [P, T]), ("av", [P, T]), ("drv", [P, T]), ("hs", [P, T]), ("o", [P, T]), ("sp4", [P, 16])]:
        C[n] = ar("C_" + n, s)
    ar = Area(D0 + 16384, M0)
    E = {}
    for n, s in [("qk", [P, 2, T]), ("qks", [P, 2, T]), ("v", [P, T]), ("fg", [P, 2, T]), ("rqk", [P, 2, T]), ("vtok", [P, 2, P]),
                 ("z", [P, 2, T]), ("cb", [P, 2, T]), ("o", [P, T])]:
        E[n] = ar("E_" + n, s)
    ar = Area(S0, END)
    for n, s in [("pT", [P, 384]), ("mask", [P, 2, T]), ("mx", [P, 2]), ("sm", [P, 2]), ("ccol", [P, 2, 8]), ("rm", [8, T])]:
        E[n] = ar("E_" + n, s)
    for n in ["f", "e", "l", "c"]:
        E[n] = ar("E_r" + n, [8, T])
    ar = Area(S0 + 16384, END)
    G = {}
    for n, s, dt in [("sg", [P, 2, T], F32), ("po", [P, 2, T], F32), ("ph", [P, 2, T], F32R), ("pl", [P, 2, T], F32R)]:
        G[n] = ar("G_" + n, s, dt)

    acc = nc.alloc_psum_tensor("acc", [P, 4, 512], F32)
    wk = nc.alloc_psum_tensor("wk", [P, 4, 512], F32)

    ada_used = nc.alloc_semaphore("ada_used")
    side_clear = nc.alloc_semaphore("side_clear")
    ada_sum = nc.alloc_semaphore("ada_sum")
    x_in = nc.alloc_semaphore("x_in")
    vec_in = nc.alloc_semaphore("vec_in")
    constA_in = nc.alloc_semaphore("constA_in")
    s5_in = nc.alloc_semaphore("s5_in")
    constB_in = nc.alloc_semaphore("constB_in")
    constR_in = nc.alloc_semaphore("constR_in")
    constC_in = nc.alloc_semaphore("constC_in")
    wab_in = nc.alloc_semaphore("wab_in")
    constE_in = nc.alloc_semaphore("constE_in")
    constP_in = nc.alloc_semaphore("constP_in")
    hi_ready = nc.alloc_semaphore("hi_ready")
    lo_ready = nc.alloc_semaphore("lo_ready")
    chunk_done = nc.alloc_semaphore("chunk_done")
    evac_done = nc.alloc_semaphore("evac_done")
    rms_sq = nc.alloc_semaphore("rms_sq")
    rms_sum = nc.alloc_semaphore("rms_sum")
    rms_var = nc.alloc_semaphore("rms_var")
    rms_sd = nc.alloc_semaphore("rms_sd")
    rms_inv = nc.alloc_semaphore("rms_inv")
    rms_scaled = nc.alloc_semaphore("rms_scaled")
    rms_affine_done = nc.alloc_semaphore("rms_affine_done")
    rms_hi = nc.alloc_semaphore("rms_hi")
    rms_lo = nc.alloc_semaphore("rms_lo")
    mod_ready = nc.alloc_semaphore("mod_ready")
    c_ready = nc.alloc_semaphore("c_ready")
    s5a_exp = nc.alloc_semaphore("s5a_exp")
    s5b_frac = nc.alloc_semaphore("s5b_frac")
    s5c_sin = nc.alloc_semaphore("s5c_sin")
    s5_ready = nc.alloc_semaphore("s5_ready")
    sc_done = nc.alloc_semaphore("sc_done")
    zm_ready = nc.alloc_semaphore("zm_ready")
    soft_ready = nc.alloc_semaphore("soft_ready")
    spm_ready = nc.alloc_semaphore("spm_ready")
    cum_done = nc.alloc_semaphore("cum_done")
    arg_ready = nc.alloc_semaphore("arg_ready")
    w_ready = nc.alloc_semaphore("w_ready")
    wm_ready = nc.alloc_semaphore("wm_ready")
    vt_done = nc.alloc_semaphore("vt_done")
    vtok_ready = nc.alloc_semaphore("vtok_ready")
    pv_done = nc.alloc_semaphore("pv_done")
    yh_ready = nc.alloc_semaphore("yh_ready")
    yl_ready = nc.alloc_semaphore("yl_ready")
    du_ready = nc.alloc_semaphore("du_ready")
    tab_step = nc.alloc_semaphore("tab_step")
    frac_ready = nc.alloc_semaphore("frac_ready")
    sin_ready = nc.alloc_semaphore("sin_ready")
    bu_done = nc.alloc_semaphore("bu_done")
    bu_used = nc.alloc_semaphore("bu_used")
    cm_ready = nc.alloc_semaphore("cm_ready")
    srot_ready = nc.alloc_semaphore("srot_ready")
    cmm_done = nc.alloc_semaphore("cmm_done")
    y5_ready = nc.alloc_semaphore("y5_ready")
    sg_ready = nc.alloc_semaphore("sg_ready")
    sg_used = nc.alloc_semaphore("sg_used")
    y_split = nc.alloc_semaphore("y_split")
    gelu_done = nc.alloc_semaphore("gelu_done")
    glu_ready = nc.alloc_semaphore("glu_ready")
    row_in = nc.alloc_semaphore("row_in")
    row_d = nc.alloc_semaphore("row_d")
    row_a = nc.alloc_semaphore("row_a")
    row_t = nc.alloc_semaphore("row_t")
    row_done = nc.alloc_semaphore("row_done")
    conv_ready = nc.alloc_semaphore("conv_ready")
    qk_ready = nc.alloc_semaphore("qk_ready")
    rm_ready = nc.alloc_semaphore("rm_ready")
    bc_done = nc.alloc_semaphore("bc_done")
    dm_arg = nc.alloc_semaphore("dm_arg")
    dm_ready = nc.alloc_semaphore("dm_ready")
    stm_ready = nc.alloc_semaphore("stm_ready")
    den_done = nc.alloc_semaphore("den_done")
    num_done = nc.alloc_semaphore("num_done")
    emt_ready = nc.alloc_semaphore("emt_ready")
    bvt_done = nc.alloc_semaphore("bvt_done")
    bvtok_ready = nc.alloc_semaphore("bvtok_ready")
    bsc_done = nc.alloc_semaphore("bsc_done")
    bsc_used = nc.alloc_semaphore("bsc_used")
    by_ready = nc.alloc_semaphore("by_ready")
    mg_split = nc.alloc_semaphore("mg_split")
    ot_used = nc.alloc_semaphore("ot_used")
    lgt_done = nc.alloc_semaphore("lgt_done")
    rt_d = nc.alloc_semaphore("rt_d")
    rt_a = nc.alloc_semaphore("rt_a")
    gt_done = nc.alloc_semaphore("gt_done")
    gT_ready = nc.alloc_semaphore("gT_ready")
    gb_rm = nc.alloc_semaphore("gb_rm")
    gb_done = nc.alloc_semaphore("gb_done")
    hid_split = nc.alloc_semaphore("hid_split")
    hid_t = nc.alloc_semaphore("hid_t")
    c0_d = nc.alloc_semaphore("c0_d")
    c0_a = nc.alloc_semaphore("c0_a")
    c0_p = nc.alloc_semaphore("c0_p")
    c_d = nc.alloc_semaphore("c_d")
    c_a = nc.alloc_semaphore("c_a")
    c_p = nc.alloc_semaphore("c_p")
    d_d = nc.alloc_semaphore("d_d")
    d_a = nc.alloc_semaphore("d_a")
    d_p = nc.alloc_semaphore("d_p")
    rowf_d = nc.alloc_semaphore("rowf_d")
    rowf_t = nc.alloc_semaphore("rowf_t")
    rowf_a = nc.alloc_semaphore("rowf_a")
    vo_d = nc.alloc_semaphore("vo_d")
    vo_a = nc.alloc_semaphore("vo_a")
    vo_m = nc.alloc_semaphore("vo_m")
    vo_ch = nc.alloc_semaphore("vo_ch")
    vb_ch = nc.alloc_semaphore("vb_ch")
    vb_conv = nc.alloc_semaphore("vb_conv")
    vo_s = nc.alloc_semaphore("vo_s")
    vo_h = nc.alloc_semaphore("vo_h")
    vo_l = nc.alloc_semaphore("vo_l")
    load = [nc.alloc_semaphore(f"load{k}") for k in range(4)]
    ADA_TURNS = NADA // 4
    C0_D = 29
    NC_D, NC_A, C_UC, C_QN, C_P, C_PT = 42, 13, 6, 9, 27, 12
    ND_D, ND_A, D_QN, D_P, D_PT = 19, 5, 9, 16, 5

    block_cm = nc.Block()
    block = block_cm.__enter__()

    @block.sync
    def _(sp):
        for k in range(4):
            sp.dma_start(stage[:, k, :], dr["ada"][k]).then_inc(load[k], 16)
        with sp.Fori(1, ADA_TURNS) as i:
            for k in range(4):
                sp.wait_ge(ada_used, i * 4 + (k - 3))
                sp.dma_start(stage[:, k, :], dr["ada"][i * 4 + k]).then_inc(load[k], 16)
        for k in range(4):
            sp.wait_ge(ada_used, NADA - 3 + k)
            sp.dma_start(stage[:, k, :], dr["main"][k]).then_inc(load[k], 16)

        def put(k, n):
            sp.wait_ge(hi_ready, n - 3)
            sp.wait_ge(lo_ready, n - 3)
            sp.dma_start(stage[:, k, :], dr["main"][n]).then_inc(load[k], 16)

        with sp.Fori(1, NMAIN // 4) as i:
            for k in range(4):
                put(k, i * 4 + k)
        for n in range(NMAIN // 4 * 4, NMAIN):
            put(n % 4, n)
        for g in range(4):
            sp.wait_ge(ot_used, 16 + 16 + ROUNDS * 16 + 4 * g + 4)
            sp.dma_start(dr["out"][:, 4 * g:4 * g + 4, :], x[:, 4 * g:4 * g + 4, :]).then_inc(x_in, 16)
        sp.wait_ge(x_in, 16 * 5)


    def each(eng, base, n, step, i0=0):
        full = n // 4
        if full > 1:
            with eng.Fori(0, full) as i:
                for j in range(4):
                    step(*slot(base + j, i), i * 4 + j)
        elif full:
            for j in range(4):
                step(*slot(base + j), j)
        for j in range(full * 4, n):
            step(*slot(base + j), j)

    def heads(eng, body):
        body(0, None)
        with eng.Fori(1, 8) as i:
            body(i, i - 1)
        body(None, 7)

    def mixed(eng, base, main, side, peel=0, side_first=False):
        def turn(u):
            for j in (2, 3, 0, 1) if side_first else range(4):
                (side if j >= 2 else main)(*slot(base + j, u), u * 2 + j % 2)
        for u in range(peel):
            turn(u)
        with eng.Fori(peel, 8) as u:
            turn(u)

    @block.gpsimd
    def _(pool):
        def low(k, q, t=None):
            n = q * 4 + k
            pool.wait_ge(hi_ready, n + 1)
            if not isinstance(n, int) or n >= 2:
                pool.wait_ge(chunk_done, n - 1)
            pool.tensor_tensor(w_lo[:, k % 2, :], stage[:, k, :], w_hi[:, k, :].bitcast(F32),
                               ALU.subtract).then_inc(lo_ready, 1)

        def passed(n0):
            def step(k, q, t):
                pool.wait_ge(ada_used, t + (n0 + 1))
                pool.wait_ge(lo_ready, q * 4 + k)
                pool.tensor_tensor(no_lo[:], ones[:, 0:8], ones[:, 0:8], ALU.subtract).then_inc(lo_ready, 1)
            return step

        for k in range(4):
            low(k, 0)
        at = 4
        for v, name in enumerate(["g_sb", "g_s5", "g_ml"]):
            each(pool, at, BASE[name] - at, low)
            mixed(pool, BASE[name], low, passed(NADA + 16 * v))
            at = BASE[name] + 32
        each(pool, at, NMAIN - at, low)

    @block.tensor
    def _(pe):
        def mm(o, w, r, start=True, stop=True):
            return pe.matmul(o, w, r, start=start, stop=stop)

        def chunk(k, q, cols, kts, ah, al, mid=None, split=None):
            n = q * 4 + k
            pe.wait_ge(hi_ready, n + 1)
            if not (isinstance(n, int) and n < 4):
                pe.wait_ge(evac_done, n - 3)
            for c in range(cols):
                o = acc[:, k, c * T:(c + 1) * T]
                for t in range(kts):
                    if split is not None and t % 4 == 0:
                        pe.wait_ge(rms_lo, split + t // 4 + 1)
                    w = w_hi[:, k, (c * kts + t) * P:(c * kts + t + 1) * P]
                    mm(o, w, ah[:, t, :], t == 0, False)
                    mm(o, w, al[:, t, :], False, False)
                if mid:
                    mid()
                if c == 0:
                    pe.wait_ge(lo_ready, n + 1)
                for t in range(kts):
                    last = mm(o, w_lo[:, k % 2, (c * kts + t) * P:(c * kts + t + 1) * P], ah[:, t, :],
                              False, t == kts - 1)
            last.then_inc(chunk_done, 1)

        def wide(k, q, t=None, mid=None, split=None):
            chunk(k, q, 1, DT, xh, xl, mid, split)

        def beside(n, g, s, work):
            if g is not None:
                wide(*slot(n, g), mid=work if s is not None else None)
            else:
                work()

        def half(k, q, t=None):
            chunk(k, q, 2, WT, yh, yl)

        def half2(k, q, t=None):
            chunk(k, q, 2, WT, yh2, yl2)

        def deep(k, q, t=None):
            chunk(k, q, 1, DT, dh, dl)

        def channel_sum(n):
            pe.wait_ge(rms_sq, n)
            mm(wk[:, 0, 0:T], ones[:], rms_red[:]).then_inc(rms_sum, 1)

        pe.wait_ge(vec_in, 16 * 3)
        pe.wait_ge(rms_sq, 1)
        for t in range(DT):
            last = mm(wk[:, 0, 0:T], ones[:], sq1[:, t, :], t == 0, t == DT - 1)
        last.then_inc(rms_sum, 1)

        def vector_sum(v, acc_of):
            pe.wait_ge(ada_used, v * 16 + 16)
            for t in range(DT):
                last = mm(wk[:, 1, v * 16 + t:v * 16 + t + 1], acc_of[:, t * P:(t + 1) * P], ones[:, 0:1])
            last.then_inc(ada_sum, 1)

        for v in range(3):
            vector_sum(v, ada_acc[:, v % 2, :])

        def passed(k, q, t):
            mm(wk[:, 3, 0:1], ones[:], ones[:, 0:1]).then_inc(chunk_done, 1)

        base = BASE["sb"]

        def stage_a(g, s):
            def bu(j):
                m = s * 4 + j
                if j == 0:
                    pe.wait_ge(evac_done, base + s * 4 + 4)
                    pe.wait_ge(s5_in, s * 32 + 32)
                pe.wait_ge(bu_used, m + 1)
                rs = slice(32 * j, 32 * j + 32)
                mm(wk[:, 2, 0:T], A["bcur"][rs, 0, :], A["u"][rs, :])
                mm(wk[:, 2, T:2 * T], A["bcur"][rs, 1, :], A["u"][rs, :]).then_inc(bu_done, 1)

            def cmm(j):
                rs = slice(32 * j, 32 * j + 32)
                pe.wait_ge(srot_ready, s * 4 + j + 1)
                mm(wk[rs, 3, 0:T], A["cm"][:, j, 0, :], A["srot"][:, j % 2, 0, :], True, False)
                mm(wk[rs, 3, 0:T], A["cm"][:, j, 1, :], A["srot"][:, j % 2, 1, :], False, True)\
                    .then_inc(cmm_done, 1)

            if s is not None:
                pe.wait_ge(evac_done, base + s * 4 + 3)
                pe.wait_ge(yl_ready, s + 1)
                for st in range(2):
                    last = mm(wk[:, 0, st * T:(st + 1) * T], A["k"][:, st * P:(st + 1) * P], A["q"][:])
                last.then_inc(sc_done, 1)
                pe.wait_ge(y5_ready, s + 1)
                for st in range(2):
                    last = pe.transpose(wk[:, 3, T + st * P:T + (st + 1) * P], A["v"][:, st * P:(st + 1) * P], ident[:])
                last.then_inc(vt_done, 1)
                bu(0)
            if g is not None:
                wide(*slot(base, g), split=0 if s is None else None)

            def sums():
                pe.wait_ge(spm_ready, s + 1)
                mm(wk[:, 1, 0:T], A["tri"][:], A["sp"][:, 0, :], True, False)
                mm(wk[:, 1, 0:T], ones[:], A["sp"][:, 1, :], False, True)
                mm(wk[:, 1, T:2 * T], A["tri"][:], A["sp"][:, 1, :]).then_inc(cum_done, 1)

            def values():
                pe.wait_ge(wm_ready, s + 1)
                mm(wk[:, 0, 0:T], A["vtok"][:, 0, :], A["w"][:, 0, :], True, False)
                mm(wk[:, 0, 0:T], A["vtok"][:, 1, :], A["w"][:, 1, :], False, True).then_inc(pv_done, 1)

            if s is not None:
                bu(1)
            beside(base + 1, g, s, sums)
            if s is not None:
                pe.wait_ge(vtok_ready, s + 1)
                cmm(0)
                bu(2)
            if g is not None:
                wide(*slot(base + 2, g))
            if s is not None:
                cmm(1)
                bu(3)
                values()
            beside(base + 3, g, s, lambda: cmm(2))
            if s is not None:
                cmm(3)

        heads(pe, stage_a)

        pe.wait_ge(yl_ready, 9)
        pe.wait_ge(yh_ready, 8)
        each(pe, BASE["p_sb"], 8, half)
        mixed(pe, BASE["g_sb"], wide, passed)
        vector_sum(3, side_acc[0])
        pe.wait_ge(y_split, 1)
        each(pe, BASE["glu"], 4, half)
        pe.wait_ge(y_split, 2)
        each(pe, BASE["p_s5"], 8, half)
        mixed(pe, BASE["g_s5"], wide, passed)
        vector_sum(4, side_acc[0])

        each(pe, BASE["mlif"], 1, wide)
        pe.wait_ge(row_d, 6)
        for st in range(2):
            last = pe.transpose(wk[:, 0, 4 * st:4 * st + 4], B["g"][0:4, st * P:(st + 1) * P], ident[0:4, 0:4])
        last.then_inc(row_t, 1)
        pe.wait_ge(row_done, 1)
        base_b = BASE["ml"]

        def stage_b(g, s):
            if s is not None:
                pe.wait_ge(qk_ready, s * 4 + 4)
                pe.wait_ge(bsc_used, s + 1)
                for st in range(2):
                    for dt in range(2):
                        last = mm(wk[:, 0, st * T:(st + 1) * T], B["qk"][:, 2 + dt, st * P:(st + 1) * P],
                                  B["qk"][:, dt, :], dt == 0, dt == 1)
                last.then_inc(bsc_done, 1)
                pe.wait_ge(rm_ready, s + 1)
                mm(wk[:, 1, :], ones[0:4, :], B["rm"][0:4, :, :]).then_inc(bc_done, 1)
                pe.wait_ge(evac_done, base_b + s * 8 + 6)
                for st in range(2):
                    for dt in range(2):
                        last = pe.transpose(wk[:, 2, st * T + dt * P:st * T + (dt + 1) * P],
                                            B["v"][:, dt, st * P:(st + 1) * P], ident[:])
                last.then_inc(bvt_done, 1)
            for j in range(8):
                if g is not None:
                    wide(*slot(base_b + j, g, 2))
                if j == 1 and s is not None:
                    pe.wait_ge(stm_ready, s + 1)
                    pe.wait_ge(bvtok_ready, s + 1)
                    for st in range(2):
                        last = mm(wk[:, 2, 0:T], ones[:], B["stm"][:, st, :], st == 0, st == 1)
                    last.then_inc(den_done, 1)
                    for dt in range(2):
                        for st in range(2):
                            last = mm(wk[:, 3, dt * T:(dt + 1) * T], B["vtok"][:, st, dt * P:(dt + 1) * P],
                                      B["stm"][:, st, :], st == 0, st == 1)
                    last.then_inc(num_done, 1)

        stage_b(0, None)
        with pe.Fori(1, 4) as i:
            stage_b(i, i - 1)
        stage_b(None, 3)
        pe.wait_ge(by_ready, 4)
        each(pe, BASE["p_ml"], 8, half)
        mixed(pe, BASE["g_ml"], wide, passed)
        vector_sum(5, side_acc[1])
        pe.wait_ge(mg_split, 1)
        each(pe, BASE["wout"], 16, deep)
        channel_sum(2)

        wide(*slot(BASE["router"]), split=4)
        pe.wait_ge(evac_done, BASE["router"] + 1)
        for tt in range(2):
            last = pe.transpose(wk[:, 0, 64 * tt:64 * tt + 64], R["lg"][0:64, tt * P:(tt + 1) * P], ident[0:64, 0:64])
        last.then_inc(lgt_done, 1)
        pe.wait_ge(rt_d, 26)
        for tt in range(2):
            last = pe.transpose(wk[0:32, 1, tt * P:(tt + 1) * P], R["gates"][:, tt, :, :], ident[:])
        last.then_inc(gt_done, 1)
        pe.wait_ge(gT_ready, 1)
        base_m = BASE["moe"]
        with pe.Fori(0, ROUNDS) as r:
            with pe.Fori(0, 8) as e:
                for j in range(4):
                    if j == 1:
                        pe.wait_ge(gb_rm, r * 8 + e + 1)
                        pe.wait_ge(hid_split, r * 16 + e * 2 + 1)
                        mm(wk[:, 0, 0:T], ones[0:32, :], R["rm"][:, :]).then_inc(gb_done, 1)
                    k, q = slot(base_m + j)
                    wide(k, r * 12 + e + q)
            with pe.Fori(0, 4) as c:
                for j in range(4):
                    if j == 0:
                        pe.wait_ge(hid_split, r * 16 + 17)
                    k, q = slot(base_m + 32 + j)
                    deep(k, r * 12 + c + q)
        channel_sum(3)
        channel_sum(4)

        for c in range(4):
            wide(*slot(BASE["kv"] + c), split=8 if c == 0 else None)
        each(pe, BASE["kv"] + 4, 8, wide)
        each(pe, BASE["bf"], 1, wide)
        pe.wait_ge(c0_d, 15)
        for j in range(2):
            last = mm(wk[:, j, :], ones[:], C["kvsq"][:, 2 * j:2 * j + 2, :])
        last.then_inc(c0_p, 1)
        pe.wait_ge(evac_done, BASE["bf"] + 1)
        for i, src in enumerate([6, 7, 10, 11]):
            for st in range(2):
                last = pe.transpose(wk[:, 2 + i // 2, (i % 2) * 256 + st * P:(i % 2) * 256 + (st + 1) * P],
                                    C["kvraw"][:, src, st * P:(st + 1) * P], ident[:])
        last.then_inc(c0_p, 1)
        pe.wait_ge(c0_d, 16)
        for tt in range(2):
            last = pe.transpose(wk[:, 0, 64 * tt:64 * tt + 24], C["bf"][0:24, tt * P:(tt + 1) * P], ident[0:24, 0:24])
        last.then_inc(c0_p, 1)
        for kv in range(2):
            if kv:
                pe.wait_ge(c0_d, 13)
                pe.wait_ge(c0_a, 3)
            xrh, xrl = (C["vrh"], C["vrl"]) if kv else (C["xrh"], C["xrl"])
            o = wk[0:32, 1 - kv, 0:T]
            for c in range(4):
                n = BASE["cmp"] + kv * 4 + c
                k = n % 4
                pe.wait_ge(hi_ready, n + 1)
                for t in range(8):
                    w = w_hi[:, k, t * T:(t + 1) * T]
                    mm(o, xrh[:, c * 8 + t, :], w, c == 0 and t == 0, False)
                    mm(o, xrl[:, c * 8 + t, :], w, False, False)
                pe.wait_ge(lo_ready, n + 1)
                for t in range(8):
                    last = mm(o, xrh[:, c * 8 + t, :], w_lo[:, k % 2, t * T:(t + 1) * T], False, c == 3 and t == 7)
                last.then_inc(chunk_done, 1)
        pe.wait_ge(evac_done, BASE["cmp"] + 4)
        for i in range(4):
            last = pe.transpose(wk[:, 1, T + 32 * i:T + 32 * i + 32], hid_rows[:, i // 2, (i % 2) * P:(i % 2 + 1) * P],
                                ident[0:32, 0:32])
        last.then_inc(hid_t, 1)
        pe.wait_ge(evac_done, BASE["cmp"] + 8)
        pe.wait_ge(constC_in, 16 * 4)
        for j in range(2):
            mm(wk[:, 2, 0:32], C["cw2"][:, j, :], C["hidc"][:, j, :], j == 0, j == 1)
        for kv in range(2):
            for j in range(2):
                last = mm(wk[0:16, 3, kv * P:(kv + 1) * P], C["hidc"][:, 2 + j, kv * 16:kv * 16 + 16], C["cw2"][:, 2 + j, :],
                          j == 0, j == 1)
        last.then_inc(c0_p, 1)
        pe.wait_ge(c0_d, 21)
        mm(wk[:, 0, 0:32], ones[:], C["kvsq"][:, 0, 0:32]).then_inc(c0_p, 1)

        base_c = BASE["nsa"]

        def stage_c(g, s, kv):
            def gates():
                pe.wait_ge(wab_in, s * 16 + 16)
                pe.wait_ge(c_d, s * NC_D + C_UC)
                for j in range(2):
                    last = mm(wk[:, 2, j * T:(j + 1) * T], C["wab"][:, j, :], C["uc"][:])
                last.then_inc(c_p, 1)

            def probs():
                pe.wait_ge(c_d, s * NC_D + C_P)
                for i in range(2):
                    for st, tt in ((0, 0), (0, 1), (1, 1)):
                        pe.transpose(wk[:, i, (st + tt) * P:(st + tt + 1) * P], C["z"][:, 2 * i + tt, st * P:(st + 1) * P], ident[:])
                for tt in range(2):
                    last = pe.transpose(wk[0:16, tt, 384:512], C["zc"][:, tt, :], ident[:])
                last.then_inc(c_p, 1)

            def values():
                pe.wait_ge(c_a, s * NC_A + C_PT)
                o = wk[:, 3, 0:T]
                for i in range(2):
                    mm(o, C["vtok"][:, 2 * i + kv, 0, :], C["pT"][:, i, 0:T], i == 0, False)
                    pe.matmul(wk[:, 3, P:T], C["vtok"][:, 2 * i + kv, 1, :], C["pT"][:, i, T:T + P], start=False, stop=False,
                              skip_group_check=True)
                mm(o, C["vct"][:, kv, :], C["pcT"][:, :], False, True).then_inc(c_p, 1)

            if s is not None:
                pe.wait_ge(c_d, s * NC_D + 1)
                mm(wk[:, 3, T:2 * T], ones[:], C["qs"][:]).then_inc(c_p, 1)
            if g is not None:
                wide(*slot(base_c, g))
            if s is not None:
                pe.wait_ge(c_d, s * NC_D + C_QN)
                for i in range(2):
                    for tt in range(2):
                        mm(wk[:, i, tt * T:(tt + 1) * T], C["qn"][:, tt * P:(tt + 1) * P], C["ks"][:, 2 * i + kv, :])
                for tt in range(2):
                    last = mm(wk[:, 3, T + 16 * tt:T + 16 * tt + 16], C["qn"][:, tt * P:(tt + 1) * P], C["kcn"][:, kv, :])
                last.then_inc(c_p, 1)
            beside(base_c + 1, g, s, gates)
            beside(base_c + 2, g, s, probs)
            beside(base_c + 3, g, s, values)

        stage_c(0, None, 0)
        with pe.Fori(1, 5) as i:
            stage_c(i, i - 1, 0)
        with pe.Fori(5, 8) as i:
            stage_c(i, i - 1, 1)
        stage_c(None, 7, 1)
        pe.wait_ge(c_d, 8 * NC_D)
        each(pe, BASE["p_a"], 8, half)
        each(pe, BASE["g_a"], 16, wide)
        each(pe, BASE["p_b"], 8, half2)
        each(pe, BASE["g_b"], 16, wide)

        base_d = BASE["fox"]
        pe.wait_ge(rowf_d, 2)
        for tt in range(2):
            last = pe.transpose(wk[:, 0, 8 * tt:8 * tt + 8], E["c"][:, tt * P:(tt + 1) * P], ident[0:8, 0:8])
        last.then_inc(rowf_t, 1)
        pe.wait_ge(rowf_d, 3)

        def stage_d(g, s):
            def scores():
                pe.wait_ge(d_d, s * ND_D + D_QN)
                for tt in range(2):
                    last = mm(wk[:, 0, tt * T:(tt + 1) * T], E["qk"][:, 0, tt * P:(tt + 1) * P], E["qk"][:, 1, :])
                last.then_inc(d_p, 1)

            def probs():
                pe.wait_ge(d_d, s * ND_D + D_P)
                for st, tt in ((0, 0), (0, 1), (1, 1)):
                    last = pe.transpose(wk[:, 1, (st + tt) * P:(st + tt + 1) * P], E["z"][:, tt, st * P:(st + 1) * P], ident[:])
                last.then_inc(d_p, 1)

            def values():
                pe.wait_ge(d_a, s * ND_A + D_PT)
                mm(wk[:, 3, 0:P], E["vtok"][:, 0, :], E["pT"][:, 0:P])
                mm(wk[:, 3, P:T], E["vtok"][:, 0, :], E["pT"][:, P:T], True, False)
                mm(wk[:, 3, P:T], E["vtok"][:, 1, :], E["pT"][:, T:T + P], False, True).then_inc(d_p, 1)

            if s is not None:
                pe.wait_ge(d_d, s * ND_D + 2)
                mm(wk[:, 1, :], ones[:], E["qks"][:]).then_inc(d_p, 1)
                pe.wait_ge(evac_done, base_d + s * 4 + 3)
                mm(wk[:, 2, 0:T], ones[0:8, :], E["rm"][:, :])
                for st in range(2):
                    last = pe.transpose(wk[:, 3, T + st * P:T + (st + 1) * P], E["v"][:, st * P:(st + 1) * P], ident[:])
                last.then_inc(d_p, 1)
            if g is not None:
                wide(*slot(base_d, g))
            beside(base_d + 1, g, s, scores)
            beside(base_d + 2, g, s, probs)
            beside(base_d + 3, g, s, values)

        heads(pe, stage_d)
        pe.wait_ge(d_d, 8 * ND_D)
        each(pe, BASE["p_c"], 8, half)
        each(pe, BASE["g_c"], 16, wide)
        pe.wait_ge(mg_split, 2)
        each(pe, BASE["wout2"], 16, deep)
        pe.wait_ge(y_split, 3)
        for c in range(2):
            n = BASE["ple"] + c
            k = n % 4
            pe.wait_ge(hi_ready, n + 1)
            pe.wait_ge(lo_ready, n + 1)
            pe.wait_ge(evac_done, n)
            for m in range(8):
                o = wk[:, m // 2, (m % 2) * T:(m % 2 + 1) * T]
                for t in range(2):
                    cs = slice((m * 2 + t) * P, (m * 2 + t + 1) * P)
                    mm(o, w_hi[:, k, cs], G["ph"][:, t, :], t == 0, False)
                    mm(o, w_hi[:, k, cs], G["pl"][:, t, :], False, False)
                    last = mm(o, w_lo[:, k % 2, cs], G["ph"][:, t, :], False, t == 1)
            last.then_inc(chunk_done, 1)
        for c in range(16):
            if c == 3:
                channel_sum(5)
            wide(*slot(BASE["pgate"] + c), split=12 if c == 0 else None)


    @block.scalar
    def _(act):
        def fn(o, i, f, **kw):
            return act.activation(o, i, f, **kw)

        def col(name, i=0):
            if isinstance(i, int):
                return vec[:, VC[name] + i:VC[name] + i + 1]
            return vec[:, ds(i + VC[name], 1)]

        def high(k, q):
            act.wait_ge(load[k], (q + ADA_TURNS) * 16 + 16)
            fn(w_hi[:, k, :], stage[:, k, :], ACT.Copy).then_inc(hi_ready, 1)

        def step(k, q, evac, more=True):
            act.wait_ge(chunk_done, q * 4 + k + 1)
            evac()
            if more:
                high(k, q + 1)

        def to(o, k, f=ACT.Identity, cols=1, **kw):
            def go():
                fn(o, acc[:, k, 0:cols * T], f, **kw).then_inc(evac_done, 1)
            return go

        act.dma_start(x[:], dr["x"]).then_inc(x_in, 16)
        act.dma_start(vec[:], dr["vec"]).then_inc(vec_in, 16)
        act.dma_start(ident[:], dr["ident"]).then_inc(vec_in, 16)
        act.dma_start(ones[:], dr["ones"]).then_inc(vec_in, 16)
        act.dma_start(A["mask"][:], dr["mask_strict"]).then_inc(constA_in, 16)
        act.dma_start(A["iota"][:], dr["iota"]).then_inc(constA_in, 16)

        def load_s5(i):
            act.dma_start(A["bcur"][:], dr["s5_b"][i]).then_inc(s5_in, 16)
            act.dma_start(A["craw"][:], dr["s5_c"][i]).then_inc(s5_in, 16)

        act.wait_ge(x_in, 16)
        for g in range(4):
            last = fn(sq1[:, 4 * g:4 * g + 4, :], x[:, 4 * g:4 * g + 4, :], ACT.Square)
        last.then_inc(rms_sq, 1)
        act.wait_ge(vec_in, 48)
        fn(cact[:], vec[:, VC["c"]:VC["c"] + 16], ACT.Silu).then_inc(c_ready, 1)

        def rms_root(c):
            act.wait_ge(rms_var, c)
            fn(rinv[:], rinv[:], ACT.Sqrt).then_inc(rms_sd, 1)

        rms_root(1)
        sp = A["s5p"]
        fn(sp[:, 0, :], vec[:, VC["log_dt"]:VC["log_dt"] + 32], ACT.Exp).then_inc(s5a_exp, 1)
        act.wait_ge(s5b_frac, 1)
        fn(sp[:, 3, :], sp[:, 1, :], ACT.Exp).then_inc(s5a_exp, 1)
        act.wait_ge(s5b_frac, 2)
        fn(sp[:, 6, :], sp[:, 4, :], ACT.Sin, scale=TWO_PI).then_inc(s5c_sin, 1)
        fn(sp[:, 7, :], sp[:, 5, :], ACT.Sin, scale=-TWO_PI, bias=col("quarter")).then_inc(s5c_sin, 1)

        def rms_affine(c, dst, scale, shift=None):
            for g in range(4):
                act.wait_ge(rms_scaled, 4 * c - 3 + g)
                for t in range(4 * g, 4 * g + 4):
                    kw = {"bias": shift(t)} if shift else {}
                    fn(dst[:, t, :], hb[:, t, :], ACT.Identity, scale=scale(t), **kw).then_inc(rms_affine_done, 1)

        def affine_split(c, n0, scale, shift=None):
            for g in range(4):
                act.wait_ge(rms_scaled, 4 * c - 3 + g)
                for t in range(4 * g, 4 * g + 4):
                    kw = {"bias": shift(t)} if shift else {}
                    fn(hb[:, t, :], hb[:, t, :], ACT.Identity, scale=scale(t), **kw).then_inc(rms_affine_done, 1)
                act.wait_ge(rms_affine_done, n0 + 4 * g + 4)
                fn(xh[:, 4 * g:4 * g + 4, :], hb[:, 4 * g:4 * g + 4, :], ACT.Copy).then_inc(rms_hi, 1)

        act.wait_ge(mod_ready, 2)
        affine_split(1, 0, lambda t: a1[:, t:t + 1], lambda t: mod[:, t:t + 1])
        for k in range(4):
            high(k, 0)
        act.wait_ge(rms_lo, 4)
        act.dma_start(A["tri"][:], dr["tri"]).then_inc(constA_in, 16)
        load_s5(0)

        base = BASE["sb"]

        def stage_a(g, s):
            if s is not None:
                act.wait_ge(zm_ready, s + 1)
                fn(A["soft"][:], A["zm"][:], ACT.Abs).then_inc(vo_a, 1)
                act.wait_ge(vo_a, s * 2 + 1)
                fn(A["soft"][:], A["soft"][:], ACT.Exp, scale=-1.0).then_inc(vo_a, 1)
                act.wait_ge(vo_a, s * 2 + 2)
                fn(A["soft"][:], A["soft"][:], ACT.Ln, bias=col("one")).then_inc(soft_ready, 1)
                act.wait_ge(vt_done, s + 1)
                fn(A["vtok"][:], wk[:, 3, T:2 * T], ACT.Copy).then_inc(vtok_ready, 1)
            if g is not None:
                if s is not None:
                    act.wait_ge(sc_done, g)
                k, q = slot(base, g)
                step(k, q, to(A["q"][:], k))
            if s is not None:
                act.wait_ge(arg_ready, s + 1)
                fn(A["w"][:], A["w"][:], ACT.Exp).then_inc(w_ready, 1)
            if g is not None:
                k, q = slot(base + 1, g)
                step(k, q, to(A["k"][:], k))
            if g is not None:
                k, q = slot(base + 2, g)
                step(k, q, to(A["v"][:], k))
            if s is not None:
                act.wait_ge(pv_done, s + 1)
                fn(yh[:, s, :], wk[:, 0, 0:T], ACT.Copy).then_inc(yh_ready, 1)
            if g is not None:
                if s is not None:
                    act.wait_ge(bu_done, g * 4)
                    act.wait_ge(du_ready, g)
                    act.wait_ge(cm_ready, g)
                    load_s5(g)
                k, q = slot(base + 3, g)
                step(k, q, to(A["u"][:], k))
                act.wait_ge(frac_ready, g + 1)
                fn(A["sin"][:], A["sin"][:], ACT.Sin, scale=-TWO_PI)
                fn(A["cos"][:], A["cos"][:], ACT.Sin, scale=-TWO_PI, bias=col("quarter")).then_inc(sin_ready, 1)

        heads(act, stage_a)

        sg_n = [0]

        def merge_p(p, pt):
            def go(k, q, t):
                step(k, q, lambda: fn(pt[:, ds(t * 2, 2), :] if not isinstance(t, int) else pt[:, 2 * t:2 * t + 2, :],
                                      acc[:, k, :], ACT.Copy).then_inc(evac_done, 1))
            each(act, BASE[p], 8, go)

        def passed(k, q, t):
            def none():
                act.wait_ge(evac_done, q * 4 + k)
                fn(vtmp[:, 9:10], ones[:, 0:1], ACT.Copy).then_inc(evac_done, 1)
            step(k, q, none)

        def merge_g(g, sg, b2=None, side=False):
            n0 = sg_n[0]

            def go(k, q, t):
                def evac():
                    if not (isinstance(t, int) and n0 + t < 2):
                        act.wait_ge(sg_used, t + (n0 - 1))
                    kw = {} if b2 is None else {"bias": col("b2", t + b2)}
                    fn(sg[:, k % 2, :], acc[:, k, 0:T], ACT.Sigmoid, **kw).then_inc(evac_done, 1)
                step(k, q, evac)
            if side:
                mixed(act, BASE[g], go, passed, peel=1 if n0 == 0 else 0)
            else:
                each(act, BASE[g], 16, go)
            sg_n[0] += 16

        act.wait_ge(y5_ready, 9)
        merge_p("p_sb", ptmp1)
        merge_g("g_sb", A["sg"], side=True)
        act.wait_ge(y5_ready, 9)
        fn(A["y5"][:], A["y5"][:], ACT.Gelu_apprx_tanh).then_inc(gelu_done, 1)
        act.wait_ge(gelu_done, 1)
        act.wait_ge(sg_used, 16)
        fn(yh[:], A["y5"][:], ACT.Copy).then_inc(gelu_done, 1)
        for t in range(4):
            k, q = slot(BASE["glu"] + t)
            if t >= 2:
                act.wait_ge(glu_ready, t - 1)
            step(k, q, to(A["y5sg"][:, t % 2, :], k, ACT.Sigmoid, 2))
        act.wait_ge(glu_ready, 4)
        fn(yh[:], A["y5"][:], ACT.Copy).then_inc(gelu_done, 1)
        merge_p("p_s5", ptmp1)
        merge_g("g_s5", A["sg"], side=True)

        act.wait_ge(sg_used, 32)
        act.wait_ge(mod_ready, 4)
        act.dma_start(B["mask"][:], dr["mask_incl"]).then_inc(constB_in, 16)
        k, q = slot(BASE["mlif"])

        def evac_rows():
            fn(B["li"][0:4, :], acc[0:4, k, 0:T], ACT.Identity, bias=vec[0:4, VC["b_if"]:VC["b_if"] + 1]).then_inc(row_in, 1)
            fn(B["lf"][0:4, :], acc[32:36, k, 0:T], ACT.Identity, bias=vec[32:36, VC["b_if"]:VC["b_if"] + 1]).then_inc(evac_done, 1)
        step(k, q, evac_rows)
        act.wait_ge(evac_done, BASE["mlif"] + 1)
        fn(B["e"][0:4, :], B["lf"][0:4, :], ACT.Abs).then_inc(row_a, 1)
        act.wait_ge(row_a, 1)
        fn(B["e"][0:4, :], B["e"][0:4, :], ACT.Exp, scale=-1.0).then_inc(row_a, 1)
        act.wait_ge(row_a, 2)
        fn(B["l"][0:4, :], B["e"][0:4, :], ACT.Ln, bias=vec[0:4, VC["one"]:VC["one"] + 1]).then_inc(row_a, 1)
        act.wait_ge(row_d, 6)
        act.wait_ge(row_t, 1)

        base_b = BASE["ml"]

        def stage_b(g, s):
            for j in range(8):
                if s is not None and j == 0:
                    act.wait_ge(dm_arg, s + 1)
                    fn(B["dm"][:], B["dm"][:], ACT.Exp).then_inc(dm_ready, 1)
                    fn(B["emt"][:], wk[:, 1, T:2 * T], ACT.Exp).then_inc(emt_ready, 1)
                    act.wait_ge(bvt_done, s + 1)
                    fn(B["vtok"][:], wk[:, 2, :], ACT.Copy).then_inc(bvtok_ready, 1)
                if s is not None and j == 4:
                    act.wait_ge(by_ready, s + 1)
                if g is not None:
                    k, q = slot(base_b + j, g, 2)
                    if j < 4:
                        if s is not None:
                            act.wait_ge(conv_ready, s * 4 + j + 1)
                        step(k, q, to(B["raw"][:, j, 3:3 + T], k))
                    elif j < 6:
                        step(k, q, to(B["v"][:, j - 4, :], k))
                    else:
                        step(k, q, to(B["so"][:, j - 6, :], k, ACT.Sigmoid))
                    if 4 <= j:
                        i = j - 4
                        act.wait_ge(conv_ready, g * 4 + i + 1)
                        if i == 0 and s is not None:
                            act.wait_ge(bsc_done, s + 1)
                        fn(B["qk"][:, i, :], B["cv"][:, i, :], ACT.Silu).then_inc(qk_ready, 1)

        stage_b(0, None)
        with act.Fori(1, 4) as i:
            stage_b(i, i - 1)
        stage_b(None, 3)
        merge_p("p_ml", ptmp1)
        merge_g("g_ml", B["sg"], side=True)

        def wout_step(k, q, t):
            def evac():
                if not (isinstance(t, int) and t < 2):
                    act.wait_ge(ot_used, t - 1)
                fn(R["ot"][:, k % 2, :], acc[:, k, 0:T], ACT.Identity,
                   scale=mod[:, ds(t + 32, 1)] if not isinstance(t, int) else mod[:, 32 + t:33 + t]).then_inc(evac_done, 1)
            step(k, q, evac)

        for t in range(4):
            wout_step(*slot(BASE["wout"] + t), t)
        each(act, BASE["wout"] + 4, 12, lambda k, q, t: wout_step(k, q, t + 4))
        rms_root(2)
        act.wait_ge(mod_ready, 6)
        affine_split(2, 16, lambda t: a2[:, t:t + 1], lambda t: mod[:, 48 + t:49 + t])
        act.dma_start(R["tri"][:], dr["tri_small"]).then_inc(constR_in, 16)
        k, q = slot(BASE["router"])
        step(k, q, lambda: fn(R["lg"][:], acc[0:64, k, 0:T], ACT.Identity, bias=vec[0:64, VC["b_rt"]:VC["b_rt"] + 1]).then_inc(evac_done, 1))
        act.wait_ge(rt_d, 3)
        fn(R["eg"][:], R["eg"][:], ACT.Exp).then_inc(rt_a, 1)
        act.wait_ge(rt_d, 19)
        fn(R["ex"][:], R["ex"][:], ACT.Exp).then_inc(rt_a, 1)
        base_m = BASE["moe"]
        with act.Fori(0, ROUNDS) as r:
            with act.Fori(0, 8) as e:
                for j in range(4):
                    k, q = slot(base_m + j)
                    o = (R["sa"] if j % 2 == 0 else R["sb"])[:, j // 2, :]

                    def evac():
                        act.wait_ge(hid_split, r * 16 + e * 2 + 1)
                        fn(o, acc[:, k, 0:T], ACT.Silu if j % 2 == 0 else ACT.Copy).then_inc(evac_done, 1)
                    step(k, r * 12 + e + q, evac)
            with act.Fori(0, 4) as c:
                for j in range(4):
                    k, q = slot(base_m + 32 + j)
                    t = c * 4 + j

                    def evac():
                        act.wait_ge(ot_used, r * 16 + c * 4 + (j + 15))
                        fn(R["ot"][:, k % 2, :], acc[:, k, 0:T], ACT.Identity, scale=mod[:, ds(t + 80, 1)]).then_inc(evac_done, 1)
                    step(k, r * 12 + c + q, evac)
        rms_root(3)
        rms_affine(3, x, lambda t: col("g_fin", t))
        rms_root(4)
        affine_split(4, 48, lambda t: col("g_ln2", t))

        def go(k, q, t):
            b = col("b2", t + B2["kv"])
            o = C["kvraw"][:, t, :]
            step(k, q, lambda: fn(o, acc[:, k, 0:T], ACT.Identity, bias=b).then_inc(evac_done, 1))
        act.wait_ge(rms_lo, 12)
        for name, src in [("mask", "mask_neg"), ("mcmp", "mask_cmp"), ("pos", "pos"), ("cw2", "cmp_w2")]:
            act.dma_start(C[name][:], dr[src]).then_inc(constC_in, 16)
        act.dma_start(C["wab"][:], dr["lru_w"][0]).then_inc(wab_in, 16)
        each(act, BASE["kv"], 12, go)
        k, q = slot(BASE["bf"])

        def evac_bf():
            fn(C["bf"][0:24, :], acc[0:24, k, 0:T], ACT.Sigmoid, bias=vec[0:24, VC["b2"] + 12:VC["b2"] + 13])
            fn(foxf[0:8, :], acc[32:40, k, 0:T], ACT.Identity, bias=vec[32:40, VC["b2"] + 12:VC["b2"] + 13]).then_inc(evac_done, 1)
        step(k, q, evac_bf)
        act.wait_ge(c0_d, 16)
        fn(C["kvsq"][:], C["kvsq"][:], ACT.Sqrt).then_inc(c0_a, 1)
        act.wait_ge(c0_p, 2)
        fn(C["vtok"][:], wk[:, 2:4, :], ACT.Copy).then_inc(c0_a, 1)
        act.wait_ge(c0_p, 3)
        fn(C["gt"][:, 0, :], wk[:, 0, 0:24], ACT.Copy)
        fn(C["gt"][:, 1, :], wk[:, 0, 64:88], ACT.Copy).then_inc(c0_a, 1)
        fn(C["sp4"][:, 8:16], vec[:, VC["lru_lam"]:VC["lru_lam"] + 8], ACT.Abs).then_inc(c0_a, 1)
        act.wait_ge(c0_a, 4)
        fn(C["sp4"][:, 8:16], C["sp4"][:, 8:16], ACT.Exp, scale=-1.0).then_inc(c0_a, 1)
        act.wait_ge(c0_a, 5)
        fn(C["sp4"][:, 8:16], C["sp4"][:, 8:16], ACT.Ln, bias=col("one")).then_inc(c0_a, 1)
        for kv in range(2):
            for c in range(4):
                n = BASE["cmp"] + kv * 4 + c
                k, q = slot(n)
                act.wait_ge(chunk_done, n + 1)
                if c == 3:
                    for ct in range(2):
                        cs = slice(ct * P, (ct + 1) * P)
                        fn(hid_rows[:, kv, cs], wk[0:32, 1 - kv, cs], ACT.Silu).then_inc(evac_done, 1)
                high(k, q + 1)
        act.wait_ge(hid_t, 1)
        for i in range(4):
            fn(C["hidc"][:, i, :], wk[:, 1, T + 32 * i:T + 32 * i + 32], ACT.Copy).then_inc(evac_done, 1)
        act.wait_ge(c0_d, 22)
        fn(C["kvsq"][:, 0, 0:32], C["kvsq"][:, 0, 0:32], ACT.Sqrt).then_inc(c0_a, 1)

        base_c = BASE["nsa"]

        def stage_c(g, s, kv):
            if s is not None:
                act.wait_ge(c_d, s * NC_D + 2)
                fn(C["rq"][:], C["rq"][:], ACT.Sqrt).then_inc(c_a, 1)
            if g is not None:
                k, q = slot(base_c, g)
                if s is not None:
                    act.wait_ge(c_d, s * NC_D + 10)
                step(k, q, to(C["q"][:], k, bias=col("b2", g * 4 + B2["nsa"])))
            if s is not None:
                act.wait_ge(c_d, s * NC_D + 16)
                for j in range(4):
                    fn(C["z"][:, j, :], C["z"][:, j, :], ACT.Exp, bias=C["mx"][:, j:j + 1], accum_out=C["sm"][:, j:j + 1]).then_inc(c_a, 1)
                for j in range(2):
                    fn(C["zc"][:, j, :], C["zc"][:, j, :], ACT.Exp, bias=C["mx"][:, 4 + j:5 + j],
                       accum_out=C["sm"][:, 4 + j:5 + j]).then_inc(c_a, 1)
            if g is not None:
                k, q = slot(base_c + 1, g)
                b = col("b2", g * 4 + (B2["nsa"] + 1))

                def evac():
                    fn(C["ng"][:, 0, :], acc[:, k, 0:T], ACT.Identity, bias=b)
                    fn(C["ng"][:, 1, :], acc[:, k, 0:T], ACT.Sigmoid, bias=b).then_inc(evac_done, 1)
                step(k, q, evac)
            if s is not None:
                act.wait_ge(c_p, s * 5 + 3)
                fn(C["ri"][:, 0, :], wk[:, 2, 0:T], ACT.Sigmoid, bias=col("lru_ba", s)).then_inc(c_a, 1)
                fn(C["ri"][:, 1, :], wk[:, 2, T:2 * T], ACT.Sigmoid, bias=col("lru_bx", s)).then_inc(c_a, 1)
                act.wait_ge(c_a, s * NC_A + 8)
                fn(C["th"][:], C["ri"][:, 0, :], ACT.Tanh,
                   scale=C["sp4"][:, s:s + 1] if isinstance(s, int) else C["sp4"][:, ds(s, 1)]).then_inc(c_a, 1)
                if g is not None:
                    act.dma_start(C["wab"][:], dr["lru_w"][g]).then_inc(wab_in, 16)
            if g is not None:
                k, q = slot(base_c + 2, g)
                step(k, q, to(C["raw"][:, 3:3 + T], k, bias=col("b2", g * 4 + (B2["nsa"] + 2))))
            if s is not None:
                act.wait_ge(c_p, s * 5 + 4)
                fn(C["pT"][:], wk[:, 0:2, 0:384], ACT.Copy).then_inc(c_a, 1)
                fn(C["pcT"][:], wk[0:16, 0:2, 384:512], ACT.Copy).then_inc(c_a, 1)
                act.wait_ge(c_d, s * NC_D + 32)
                fn(C["sqv"][:], C["th"][:], ACT.Sqrt).then_inc(c_a, 1)
            if g is not None:
                k, q = slot(base_c + 3, g)
                b3 = col("b2", g * 4 + (B2["nsa"] + 3))

                def evac():
                    fn(C["lg"][:, 0, :], acc[:, k, 0:T], ACT.Identity, bias=b3)
                    fn(C["lg"][:, 1, :], acc[:, k, 0:T], ACT.Sigmoid, bias=b3).then_inc(evac_done, 1)
                step(k, q, evac)

        stage_c(0, None, 0)
        with act.Fori(1, 5) as i:
            stage_c(i, i - 1, 0)
        with act.Fori(5, 8) as i:
            stage_c(i, i - 1, 1)
        stage_c(None, 7, 1)
        act.wait_ge(c_d, 8 * NC_D)
        merge_p("p_a", ptmp2)
        merge_g("g_a", G["sg"], B2["g_a"])
        act.wait_ge(sg_used, 64)
        merge_p("p_b", ptmp2)
        merge_g("g_b", G["sg"], B2["g_b"])

        act.wait_ge(sg_used, 80)
        act.dma_start(E["mask"][:], dr["mask_neg"]).then_inc(constE_in, 16)
        fn(E["e"][:], foxf[0:8, :], ACT.Abs).then_inc(rowf_a, 1)
        act.wait_ge(rowf_a, 1)
        fn(E["e"][:], E["e"][:], ACT.Exp, scale=-1.0).then_inc(rowf_a, 1)
        act.wait_ge(rowf_a, 2)
        fn(E["l"][:], E["e"][:], ACT.Ln, bias=vec[0:8, VC["one"]:VC["one"] + 1]).then_inc(rowf_a, 1)
        base_d = BASE["fox"]

        def stage_d(g, s):
            if s is not None:
                act.wait_ge(d_d, s * ND_D + 3)
                fn(E["rqk"][:], E["rqk"][:], ACT.Sqrt).then_inc(d_a, 1)
                act.wait_ge(d_p, s * 5 + 2)
                fn(E["vtok"][:], wk[:, 3, T:2 * T], ACT.Copy).then_inc(d_a, 1)
            if s is not None:
                act.wait_ge(d_p, s * 5 + 3)
            if g is not None:
                k, q = slot(base_d, g)
                step(k, q, to(E["qk"][:, 0, :], k, bias=col("b2", g * 4 + B2["fox"])))
            if s is not None:
                act.wait_ge(d_d, s * ND_D + 12)
                for j in range(2):
                    fn(E["z"][:, j, :], E["z"][:, j, :], ACT.Exp, bias=E["mx"][:, j:j + 1], accum_out=E["sm"][:, j:j + 1]).then_inc(d_a, 1)
            if g is not None:
                k, q = slot(base_d + 1, g)
                step(k, q, to(E["qk"][:, 1, :], k, bias=col("b2", g * 4 + (B2["fox"] + 1))))
            if s is not None:
                act.wait_ge(d_p, s * 5 + 4)
                fn(E["pT"][:], wk[:, 1, 0:384], ACT.Copy).then_inc(d_a, 1)
            if g is not None:
                k, q = slot(base_d + 2, g)
                step(k, q, to(E["v"][:], k, bias=col("b2", g * 4 + (B2["fox"] + 2))))
                k, q = slot(base_d + 3, g)
                b = col("b2", g * 4 + (B2["fox"] + 3))

                def evac():
                    fn(E["fg"][:, 0, :], acc[:, k, 0:T], ACT.Identity, bias=b)
                    fn(E["fg"][:, 1, :], acc[:, k, 0:T], ACT.Sigmoid, bias=b).then_inc(evac_done, 1)
                step(k, q, evac)

        heads(act, stage_d)
        act.wait_ge(d_d, 8 * ND_D)
        merge_p("p_c", ptmp2)
        merge_g("g_c", G["sg"], B2["g_c"])

        act.wait_ge(mg_split, 2)
        act.dma_start(G["po"][:], dr["p"]).then_inc(constP_in, 16)
        act.wait_ge(constP_in, 16)
        fn(G["ph"][:], G["po"][:], ACT.Copy).then_inc(gelu_done, 1)
        n0 = 16 + ROUNDS * 16

        def go(k, q, t):
            def evac():
                act.wait_ge(ot_used, t + (n0 - 1))
                fn(G["sg"][:, k % 2, :], acc[:, k, 0:T], ACT.Copy).then_inc(evac_done, 1)
            step(k, q, evac)
        each(act, BASE["wout2"], 16, go)
        for g in range(4):
            act.wait_ge(ot_used, n0 + 4 * g + 4)
            fn(xh[:, 4 * g:4 * g + 4, :], x[:, 4 * g:4 * g + 4, :], ACT.Copy).then_inc(rms_hi, 1)
        for c in range(2):
            n = BASE["ple"] + c
            k, q = slot(n)
            step(k, q, lambda: fn(merged[:, 8 * c:8 * c + 8, :], wk[:, :, :], ACT.Copy).then_inc(evac_done, 1))
        def last_gate(k, q, t, more=True):
            def evac():
                act.wait_ge(ot_used, t + (n0 + 16 - 1))
                fn(G["sg"][:, k % 2, :], acc[:, k, 0:T], ACT.Sigmoid).then_inc(evac_done, 1)
            step(k, q, evac, more)
        for t in range(16):
            if t == 2:
                rms_root(5)
                rms_affine(5, merged, lambda t: col("g_ple", t))
            last_gate(*slot(BASE["pgate"] + t), t, t < 12)

    @block.vector
    def _(dve):
        def tt(o, a, b, op):
            return dve.tensor_tensor(o, a, b, op)

        def ts(o, a, s1, op0, s2=None, op1=None):
            return dve.tensor_scalar(o, a, s1, s2, op0, op1) if op1 else dve.tensor_scalar(o, a, s1, None, op0)

        def stt(o, a, s, b, op0, op1):
            return dve.scalar_tensor_tensor(out=o, in0=a, scalar=s, in1=b, op0=op0, op1=op1)

        def cp(o, a):
            return dve.tensor_copy(o, a)

        def red(o, a, op):
            return dve.tensor_reduce(o, a, AX, op)

        def vcol(name, i=0):
            if isinstance(i, int):
                return vec[:, VC[name] + i:VC[name] + i + 1]
            return vec[:, ds(i + VC[name], 1)]

        class Count:

            def __init__(self, per=0, it=0):
                self.per, self.n, self.base = per, 0, it * per if per else 0

            def next(self):
                self.n += 1
                return self.base + self.n

            def check(self):
                assert self.n == self.per, (self.n, self.per)

        MUL, ADD, SUB, MAX, MIN = ALU.mult, ALU.add, ALU.subtract, ALU.max, ALU.min
        INV2PI = 0.15915494309189535
        C1, C2, C3 = 6.28125, 0.0019350051879882812, 3.019916050561733e-07

        def rms(c, src):
            if c > 1:
                tt(sq[:], src[:], src[:], MUL).then_inc(vo_d, 1)
                dve.wait_ge(vo_d, c - 1)
                red(rms_red[:], sq[:].rearrange("p t n -> p n t"), ADD).then_inc(rms_sq, 1)
            dve.wait_ge(rms_sum, c)
            ts(rinv[:], wk[:, 0, 0:T], 1.0 / D, MUL, EPS, ADD).then_inc(rms_var, 1)
            dve.wait_ge(rms_sd, c)
            dve.reciprocal(rinv[:], rinv[:]).then_inc(rms_inv, 1)
            dve.wait_ge(rms_inv, c)
            for g in range(4):
                gs = slice(4 * g, 4 * g + 4)
                tt(hb[:, gs, :], src[:, gs, :], rinv[:].unsqueeze(1).to_broadcast([P, 4, T]), MUL).then_inc(rms_scaled, 1)

        def split_lo(src, n0):
            for g in range(4):
                gs = slice(4 * g, 4 * g + 4)
                dve.wait_ge(rms_hi, n0 + g + 1)
                tt(xl[:, gs, :], src[:, gs, :], xh[:, gs, :].bitcast(F32), SUB).then_inc(rms_lo, 1)

        def free(i, *sems):
            for n, sem in enumerate(sems):
                dve.memset(vtmp[:, i + n:i + n + 1], 0.0).then_inc(sem, 1)

        def ada(i, par):
            if i:
                dve.wait_ge(ada_sum, i * 2 + (par - 1))
            for t in range(DT):
                k = t % 4
                dve.wait_ge(load[k], i * 128 + (par * 64 + (t // 4) * 16 + 16))
                w, o, cc = stage[:, k, :], ada_acc[:, par, :], cact[:, t:t + 1]
                if t == 0:
                    ts(o, w, cc, MUL).then_inc(ada_used, 1)
                else:
                    dve.wait_ge(ada_used, i * 32 + (par * 16 + t))
                    stt(o, w, cc, o, MUL, ADD).then_inc(ada_used, 1)

        dve.wait_ge(c_ready, 1)
        ada(0, 0)
        ada(0, 1)

        rms(1, x)
        s5 = A["s5p"]
        done = Count()
        v = lambda n: vec[:, VC[n]:VC[n] + 32]
        dve.wait_ge(s5a_exp, 1)
        tt(s5[:, 1, :], v("lam_re"), s5[:, 0, :], MUL).then_inc(s5b_frac, 1)
        tt(s5[:, 2, :], v("lam_im"), s5[:, 0, :], MUL).then_inc(s5_ready, 1)
        dve.wait_ge(s5_ready, done.next())
        ts(s5[:, 8, :], s5[:, 2, :], INV2PI, MUL, MAGIC, ADD).then_inc(s5_ready, 1)
        dve.wait_ge(s5_ready, done.next())
        ts(s5[:, 8, :], s5[:, 8, :], -MAGIC, ADD).then_inc(s5_ready, 1)
        dve.wait_ge(s5_ready, done.next())
        for cst in (C1, C2, C3):
            stt(s5[:, 2, :], s5[:, 8, :], -cst, s5[:, 2, :], MUL, ADD).then_inc(s5_ready, 1)
            dve.wait_ge(s5_ready, done.next())
        ts(s5[:, 4, :], s5[:, 2, :], INV2PI, MUL).then_inc(s5_ready, 1)
        dve.wait_ge(s5_ready, done.next())
        ts(s5[:, 8, :], s5[:, 4, :], MAGIC, ADD).then_inc(s5_ready, 1)
        dve.wait_ge(s5_ready, done.next())
        stt(s5[:, 4, :], s5[:, 8, :], -MAGIC, s5[:, 4, :], ADD, SUB).then_inc(s5_ready, 1)
        dve.wait_ge(s5_ready, done.next())
        ts(s5[:, 4, :], s5[:, 4, :], -1.0, MUL).then_inc(s5_ready, 1)
        dve.wait_ge(s5_ready, done.next())
        ts(s5[:, 8, :], s5[:, 4, :], 0.25, ADD, MAGIC, ADD).then_inc(s5_ready, 1)
        dve.wait_ge(s5_ready, done.next())
        stt(s5[:, 5, :], s5[:, 8, :], -MAGIC, s5[:, 4, :], ADD, SUB).then_inc(s5_ready, 1)
        dve.wait_ge(s5_ready, done.next())
        ts(s5[:, 5, :], s5[:, 5, :], -0.25, MAX, 0.75, MIN).then_inc(s5b_frac, 1)
        dve.wait_ge(s5a_exp, 2)
        dve.wait_ge(s5c_sin, 2)
        tt(s5[:, 9, :], s5[:, 3, :], s5[:, 7, :], MUL).then_inc(s5_ready, 1)
        dve.wait_ge(s5_ready, done.next())
        ts(s5[:, 9, :], s5[:, 9, :], -1.0, ADD).then_inc(s5_ready, 1)
        dve.wait_ge(s5_ready, done.next())
        tt(s5[:, 10, :], s5[:, 3, :], s5[:, 6, :], MUL).then_inc(s5_ready, 1)
        dve.wait_ge(s5_ready, done.next())
        tt(s5[:, 11, :], v("lam_re"), v("lam_re"), MUL).then_inc(s5_ready, 1)
        dve.wait_ge(s5_ready, done.next())
        tt(s5[:, 12, :], v("lam_im"), v("lam_im"), MUL).then_inc(s5_ready, 1)
        dve.wait_ge(s5_ready, done.next())
        tt(s5[:, 11, :], s5[:, 11, :], s5[:, 12, :], ADD).then_inc(s5_ready, 1)
        dve.wait_ge(s5_ready, done.next())
        dve.reciprocal(s5[:, 11, :], s5[:, 11, :]).then_inc(s5_ready, 1)
        dve.wait_ge(s5_ready, done.next())
        tt(s5[:, 12, :], s5[:, 9, :], v("lam_re"), MUL).then_inc(s5_ready, 1)
        dve.wait_ge(s5_ready, done.next())
        tt(s5[:, 13, :], s5[:, 10, :], v("lam_im"), MUL).then_inc(s5_ready, 1)
        dve.wait_ge(s5_ready, done.next())
        tt(s5[:, 12, :], s5[:, 12, :], s5[:, 13, :], ADD).then_inc(s5_ready, 1)
        dve.wait_ge(s5_ready, done.next())
        tt(s5[:, 12, :], s5[:, 12, :], s5[:, 11, :], MUL).then_inc(s5_ready, 1)
        dve.wait_ge(s5_ready, done.next())
        tt(s5[:, 13, :], s5[:, 10, :], v("lam_re"), MUL).then_inc(s5_ready, 1)
        dve.wait_ge(s5_ready, done.next())
        tt(s5[:, 0, :], s5[:, 9, :], v("lam_im"), MUL).then_inc(s5_ready, 1)
        dve.wait_ge(s5_ready, done.next())
        tt(s5[:, 13, :], s5[:, 13, :], s5[:, 0, :], SUB).then_inc(s5_ready, 1)
        dve.wait_ge(s5_ready, done.next())
        tt(s5[:, 13, :], s5[:, 13, :], s5[:, 11, :], MUL).then_inc(s5_ready, 1)
        dve.wait_ge(s5_ready, done.next())
        ada(1, 0)
        dve.wait_ge(ada_sum, 3)
        tt(mod[:, 0:48], wk[:, 1, 0:48], vec[:, VC["b_ada"]:VC["b_ada"] + 48], ADD).then_inc(mod_ready, 1)
        dve.wait_ge(mod_ready, 1)
        stt(a1[:], mod[:, 16:32], 1.0, vec[:, VC["g_mix"]:VC["g_mix"] + 16], ADD, MUL).then_inc(mod_ready, 1)
        free(0, yl_ready, y5_ready, bu_used, bsc_used, hid_split)
        split_lo(hb, 0)

        base = BASE["sb"]
        dve.wait_ge(constA_in, 48)
        A_N = 14

        def tables(s):
            b3 = [P, 4, T]
            done = Count(5, s)
            phase = s5[:, 4, ds(s * 4, 4)].unsqueeze(2).to_broadcast(b3)
            tt(A["ph"][:], A["iota"][:].unsqueeze(1).to_broadcast(b3), phase, MUL).then_inc(tab_step, 1)
            dve.wait_ge(tab_step, done.next())
            ts(A["sin"][:], A["ph"][:], MAGIC, ADD).then_inc(tab_step, 1)
            dve.wait_ge(tab_step, done.next())
            stt(A["sin"][:], A["sin"][:], -MAGIC, A["ph"][:], ADD, SUB).then_inc(tab_step, 1)
            dve.wait_ge(tab_step, done.next())
            ts(A["cos"][:], A["ph"][:], 0.25, ADD, MAGIC, ADD).then_inc(tab_step, 1)
            dve.wait_ge(tab_step, done.next())
            stt(A["cos"][:], A["cos"][:], -MAGIC, A["ph"][:], ADD, SUB).then_inc(tab_step, 1)
            dve.wait_ge(tab_step, done.next())
            ts(A["cos"][:], A["cos"][:], -0.25, MAX, 0.75, MIN).then_inc(frac_ready, 1)

        def stage_a(g, s):
            if s is None:
                tables(0)
                return
            i32 = lambda n, k=4: s5[:, n, ds(s * 4, k)]
            done = Count(A_N, s)
            dve.wait_ge(sc_done, s + 1)
            stt(A["zm"][:], wk[:, 0, :], SB_SCALE, A["mask"][:], MUL, MUL).then_inc(zm_ready, 1)
            dve.wait_ge(s5_in, s * 32 + 32)
            b4 = [P, 4, 2, 32]
            bc = lambda n: i32(n).unsqueeze(2).to_broadcast([P, 4, 64])
            cr = A["craw"][:].rearrange("p j c h -> p j (c h)")
            tt(A["c1"][:].rearrange("p j c h -> p j (c h)"), cr, bc(12), MUL)
            tt(A["c2"][:].rearrange("p j c h -> p j (c h)"), cr, bc(13), MUL).then_inc(vo_ch, 1)
            dve.wait_ge(vo_ch, done.next())
            tt(A["cm"][:, :, 0, :], A["c1"][:, :, 0, :], A["c2"][:, :, 1, :], SUB)
            stt(A["cm"][:, :, 1, :], A["c2"][:, :, 0, :], -1.0, A["c1"][:, :, 1, :], MUL, SUB).then_inc(cm_ready, 1)
            dve.wait_ge(evac_done, base + s * 4 + 4)
            ts(A["du"][:], A["u"][:], vcol("s5_d", s), MUL).then_inc(du_ready, 1)

            def rotate(j):
                b2 = [P, 2, T]
                cos = A["cos"][:, j:j + 1, :].to_broadcast(b2)
                sin = A["sin"][:, j:j + 1, :].to_broadcast(b2)
                bu = wk[:, 2, :].rearrange("p (c t) -> p c t", c=2)
                dve.wait_ge(bu_done, s * 4 + j + 1)
                if j == 0:
                    dve.wait_ge(sin_ready, s + 1)
                else:
                    dve.wait_ge(srot_ready, s * 4 + j)
                tt(A["t1"][:], bu, cos, MUL)
                tt(A["t2"][:], bu, sin, MUL).then_inc(bu_used, 1)
                dve.wait_ge(bu_used, s * 4 + j + 2)
                tt(A["vr"][:, 0, :], A["t1"][:, 0, :], A["t2"][:, 1, :], ADD)
                tt(A["vr"][:, 1, :], A["t1"][:, 1, :], A["t2"][:, 0, :], SUB).then_inc(vo_ch, 1)
                dve.wait_ge(vo_ch, done.next())
                r = s5[:, 3, ds(s * 4 + j, 1)].to_broadcast([P, T])
                dve.tensor_tensor_scan(A["sc"][:, 0, :], r, A["vr"][:, 0, :], 0.0, MUL, ADD)
                dve.tensor_tensor_scan(A["sc"][:, 1, :], r, A["vr"][:, 1, :], 0.0, MUL, ADD).then_inc(vo_ch, 1)
                dve.wait_ge(vo_ch, done.next())
                tt(A["t1"][:], A["sc"][:], cos, MUL)
                tt(A["t2"][:], A["sc"][:], sin, MUL).then_inc(vo_ch, 1)
                dve.wait_ge(vo_ch, done.next())
                if j >= 2:
                    dve.wait_ge(cmm_done, s * 4 + j - 1)
                tt(A["srot"][:, j % 2, 0, :], A["t1"][:, 0, :], A["t2"][:, 1, :], SUB)
                tt(A["srot"][:, j % 2, 1, :], A["t2"][:, 0, :], A["t1"][:, 1, :], ADD).then_inc(srot_ready, 1)

            rotate(0)
            dve.wait_ge(zm_ready, s + 1)
            dve.wait_ge(soft_ready, s + 1)
            stt(A["sp"][:], A["zm"][:], 0.0, A["soft"][:], MAX, ADD).then_inc(vo_ch, 1)
            dve.wait_ge(vo_ch, done.next())
            tt(A["sp"][:], A["sp"][:], A["mask"][:], MUL).then_inc(spm_ready, 1)
            rotate(1)
            dve.wait_ge(cum_done, s + 1)
            tt(A["w"][:], A["zm"][:], wk[:, 1, :].rearrange("p (c t) -> p c t", c=2), SUB).then_inc(arg_ready, 1)
            rotate(2)
            dve.wait_ge(w_ready, s + 1)
            tt(A["w"][:], A["w"][:], A["mask"][:], MUL).then_inc(wm_ready, 1)
            rotate(3)
            dve.wait_ge(yh_ready, s + 1)
            tt(yl[:, s, :], wk[:, 0, 0:T], yh[:, s, :].bitcast(F32), SUB).then_inc(yl_ready, 1)
            dve.wait_ge(cmm_done, s * 4 + 4)
            tt(A["y5"][:, s, :], wk[:, 3, 0:T], A["du"][:], ADD).then_inc(y5_ready, 1)
            done.check()
            if g is not None:
                tables(g)

        heads(dve, stage_a)

        sg_n = [0]

        def merge_g(g, sg, pt, first=False, v=None, side=None):
            n0 = sg_n[0]

            def go(k, q, t):
                dve.wait_ge(evac_done, q * 4 + k + 1)
                if first:
                    tt(merged[:, t, :], sg[:, k % 2, :], pt[:, t, :], MUL).then_inc(sg_used, 1)
                else:
                    tt(sg[:, k % 2, :], sg[:, k % 2, :], pt[:, t, :], MUL).then_inc(sg_ready, 1)
                    dve.wait_ge(sg_ready, n0 + t + 1)
                    tt(merged[:, t, :], merged[:, t, :], sg[:, k % 2, :], ADD).then_inc(sg_used, 1)

            def ada_step(k, q, t):
                dve.wait_ge(load[k], (q + ADA_TURNS) * 16 + 16)
                dve.wait_ge(ada_used, t + v * 16)
                stt(side[:], stage[:, k, :], cact[:, ds(t, 1)], side[:], MUL, ADD).then_inc(ada_used, 1)

            if v is None:
                each(dve, BASE[g], 16, go)
            else:
                dve.memset(side[:], 0.0).then_inc(side_clear, 1)
                dve.wait_ge(side_clear, v - 2)
                mixed(dve, BASE[g], go, ada_step, side_first=True)
                dve.wait_ge(ada_sum, v + 1)
                cs = slice(16 * v, 16 * v + 16)
                tt(mod[:, cs], wk[:, 1, cs], vec[:, VC["b_ada"] + 16 * v:VC["b_ada"] + 16 * v + 16], ADD).then_inc(mod_ready, 1)
            if not first:
                sg_n[0] += 16

        merge_g("g_sb", A["sg"], ptmp1, True, 3, side_acc[0])
        dve.wait_ge(gelu_done, 2)
        tt(yl[:], A["y5"][:], yh[:].bitcast(F32), SUB).then_inc(y_split, 1)
        for t in range(4):
            dve.wait_ge(evac_done, BASE["glu"] + t + 1)
            o = A["y5"][:, 2 * t:2 * t + 2, :]
            tt(o, o, A["y5sg"][:, t % 2, :].rearrange("p (c t) -> p c t", c=2), MUL).then_inc(glu_ready, 1)
        dve.wait_ge(gelu_done, 3)
        tt(yl[:], A["y5"][:], yh[:].bitcast(F32), SUB).then_inc(y_split, 1)
        merge_g("g_s5", A["sg"], ptmp1, False, 4, side_acc[0])

        done = Count()
        r4 = slice(0, 4)
        one_row = lambda n: ones[0:n, 0:1].to_broadcast([n, T])
        dve.wait_ge(evac_done, BASE["mlif"] + 1)
        dve.wait_ge(row_a, 3)
        stt(B["lf"][r4, :], B["lf"][r4, :], 0.0, B["l"][r4, :], MIN, SUB).then_inc(row_d, 1)
        dve.wait_ge(row_d, done.next())
        dve.tensor_tensor_scan(B["b"][r4, :], one_row(4), B["lf"][r4, :], 0.0, MUL, ADD).then_inc(row_d, 1)
        dve.wait_ge(row_d, done.next())
        tt(B["g"][r4, :], B["li"][r4, :], B["b"][r4, :], SUB).then_inc(row_d, 1)
        dve.wait_ge(row_d, done.next())
        dve.tensor_tensor_scan(B["m"][r4, :], one_row(4), B["g"][r4, :], 0.0, MUL, MAX).then_inc(row_d, 1)
        dve.wait_ge(row_d, done.next())
        ts(B["rows"][r4, 0, :], B["m"][r4, :], -1.0, MUL).then_inc(row_d, 1)
        dve.wait_ge(row_d, done.next())
        stt(B["rows"][r4, 1, :], B["b"][r4, :], -1.0, B["m"][r4, :], MUL, SUB).then_inc(row_d, 1)
        dve.wait_ge(row_d, done.next())
        dve.wait_ge(row_t, 1)
        cp(B["gcol"][:], wk[:, 0, 0:8]).then_inc(row_done, 1)
        dve.wait_ge(row_done, 1)
        dve.memset(B["raw"][:, :, 0:3], 0.0).then_inc(vo_m, 1)
        dve.wait_ge(vo_m, 1)
        dve.wait_ge(constB_in, 16)

        base_b = BASE["ml"]
        B_N = 7

        def stage_b(g, s):
            if s is not None:
                done = Count(B_N, s)
                ts(B["rm"][r4, :, :], B["rows"][r4, :, :], ident[0:4, ds(s, 1)], MUL).then_inc(rm_ready, 1)
                dve.wait_ge(bc_done, s + 1)
                for st in range(2):
                    ins = ts(B["dm"][:, st, :], wk[:, 1, 0:T], B["gcol"][:, ds(s + 4 * st, 1)], ADD, 0.0, MIN)
                ins.then_inc(dm_arg, 1)
                dve.wait_ge(dm_ready, s + 1)
                dve.wait_ge(bsc_done, s + 1)
                stt(B["st"][:], wk[:, 0, :].rearrange("p (c t) -> p c t", c=2), ML_SCALE, B["dm"][:], MUL, MUL).then_inc(bsc_used, 1)
                dve.wait_ge(bsc_used, s + 2)
                tt(B["stm"][:], B["st"][:], B["mask"][:], MUL).then_inc(stm_ready, 1)

            def conv(j):
                n = base_b + j
                dve.wait_ge(evac_done, n + 1 + g * 8)
                w = lambda tap: vcol("conv", g * 16 + (j * 4 + tap))
                if not (isinstance(g, int) and g == 0):
                    dve.wait_ge(qk_ready, g * 4 + (j + 1 - 4))
                ts(B["cv"][:, j, :], B["raw"][:, j, 0:T], w(0), MUL).then_inc(vb_conv, 1)
                for tap in range(1, 4):
                    dve.wait_ge(vb_conv, g * 12 + (j * 3 + tap))
                    stt(B["cv"][:, j, :], B["raw"][:, j, tap:tap + T], w(tap), B["cv"][:, j, :], MUL, ADD).then_inc(vb_conv if tap < 3 else conv_ready, 1)

            if g is not None:
                conv(0)
            if s is not None:
                dve.wait_ge(den_done, s + 1)
                ts(B["ad"][:], wk[:, 2, 0:T], -1.0, MUL).then_inc(vb_ch, 1)
                dve.wait_ge(vb_ch, done.next())
                tt(B["ad"][:], wk[:, 2, 0:T], B["ad"][:], MAX).then_inc(vb_ch, 1)
                dve.wait_ge(vb_ch, done.next())
                dve.wait_ge(emt_ready, s + 1)
                tt(B["ad"][:], B["ad"][:], B["emt"][:], MAX).then_inc(vb_ch, 1)
                dve.wait_ge(vb_ch, done.next())
                dve.reciprocal(B["rec"][:], B["ad"][:]).then_inc(vb_ch, 1)
                dve.wait_ge(vb_ch, done.next())
                dve.wait_ge(num_done, s + 1)
                tt(B["y"][:], wk[:, 3, :].rearrange("p (c t) -> p c t", c=2), B["rec"][:].unsqueeze(1).to_broadcast([P, 2, T]), MUL).then_inc(vb_ch, 1)
                dve.wait_ge(vb_ch, done.next())
                tt(B["y"][:], B["y"][:], B["so"][:], MUL).then_inc(vb_ch, 1)
                dve.wait_ge(vb_ch, done.next())
                cp(yh[:, ds(s * 2, 2), :], B["y"][:]).then_inc(vb_ch, 1)
                dve.wait_ge(vb_ch, done.next())
                tt(yl[:, ds(s * 2, 2), :], B["y"][:], yh[:, ds(s * 2, 2), :].bitcast(F32), SUB).then_inc(by_ready, 1)
                done.check()
            if g is not None:
                for j in range(1, 4):
                    conv(j)

        stage_b(0, None)
        with dve.Fori(1, 4) as i:
            stage_b(i, i - 1)
        stage_b(None, 3)
        merge_g("g_ml", B["sg"], ptmp1, False, 5, side_acc[1])
        dve.wait_ge(mod_ready, 5)
        stt(a2[:], mod[:, 64:80], 1.0, vec[:, VC["g_moe"]:VC["g_moe"] + 16], ADD, MUL).then_inc(mod_ready, 1)

        def split_merged(n):
            dve.wait_ge(sg_used, 48 * n)
            cp(dh[:], merged[:]).then_inc(vo_s, 1)
            dve.wait_ge(vo_s, n)
            tt(dl[:], merged[:], dh[:].bitcast(F32), SUB).then_inc(mg_split, 1)

        def add_out(k, q, t, buf=R["ot"]):
            dve.wait_ge(evac_done, q * 4 + k + 1)
            tt(x[:, t, :], x[:, t, :], buf[:, k % 2, :], ADD).then_inc(ot_used, 1)

        split_merged(1)
        each(dve, BASE["wout"], 16, add_out)
        dve.wait_ge(ot_used, 16)
        rms(2, x)
        split_lo(hb, 4)
        done = Count()
        L = R["L"]
        dve.wait_ge(lgt_done, 1)
        dve.wait_ge(constR_in, 16)
        cp(L[:].rearrange("p a b -> p (a b)"), wk[:, 0, 0:128]).then_inc(rt_d, 1)
        dve.wait_ge(rt_d, done.next())
        Gl, El = L[:, :, 0:4], L[:, :, 32:64].rearrange("p a (g e) -> p a g e", g=4)
        red(R["gmax"][:], Gl, MAX).then_inc(rt_d, 1)
        dve.wait_ge(rt_d, done.next())
        tt(R["eg"][:], Gl, R["gmax"][:].unsqueeze(2).to_broadcast([P, 2, 4]), SUB).then_inc(rt_d, 1)
        dve.wait_ge(rt_d, done.next())

        def rank(dst, a, b, v, n, tri):
            s4 = [P, 2, n, n]
            vi, vj = v.unsqueeze(2).to_broadcast(s4), v.unsqueeze(3).to_broadcast(s4)
            tt(a[:], vi, vj, ALU.is_gt).then_inc(rt_d, 1)
            dve.wait_ge(rt_d, done.next())
            tt(b[:], vi, vj, ALU.is_equal).then_inc(rt_d, 1)
            dve.wait_ge(rt_d, done.next())
            for h in range(2):
                ins = tt(b[:, h], b[:, h], tri, MUL)
            ins.then_inc(rt_d, 1)
            dve.wait_ge(rt_d, done.next())
            tt(a[:], a[:], b[:], ADD).then_inc(rt_d, 1)
            dve.wait_ge(rt_d, done.next())
            red(dst[:], a[:], ADD).then_inc(rt_d, 1)
            dve.wait_ge(rt_d, done.next())
        rank(R["oh"], R["g4a"], R["g4b"], Gl, 4, R["tri"][:, 64:80].rearrange("p (j i) -> p j i", j=4))
        ts(R["oh"][:], R["oh"][:], 0.5, ALU.is_lt).then_inc(rt_d, 1)
        dve.wait_ge(rt_d, done.next())
        tt(R["ep"][:], El, R["oh"][:].unsqueeze(3).to_broadcast([P, 2, 4, 8]), MUL).then_inc(rt_d, 1)
        dve.wait_ge(rt_d, done.next())
        red(R["es"][:], R["ep"][:].rearrange("p a g e -> p a e g"), ADD).then_inc(rt_d, 1)
        dve.wait_ge(rt_d, done.next())
        rank(R["sel"], R["e8a"], R["e8b"], R["es"][:], 8, R["tri"][:, 0:64].rearrange("p (j i) -> p j i", j=8))
        ts(R["sel"][:], R["sel"][:], 1.5, ALU.is_lt).then_inc(rt_d, 1)
        dve.wait_ge(rt_d, done.next())
        red(R["emax"][:], R["es"][:], MAX).then_inc(rt_d, 1)
        dve.wait_ge(rt_d, done.next())
        tt(R["ex"][:], R["es"][:], R["emax"][:].unsqueeze(2).to_broadcast([P, 2, 8]), SUB).then_inc(rt_d, 1)
        dve.wait_ge(rt_d, done.next())
        assert done.n == 19, done.n
        dve.wait_ge(rt_a, 2)
        tt(R["ex"][:], R["ex"][:], R["sel"][:], MUL).then_inc(rt_d, 1)
        dve.wait_ge(rt_d, done.next())
        red(R["esum"][:], R["ex"][:], ADD).then_inc(rt_d, 1)
        dve.wait_ge(rt_d, done.next())
        red(R["gsum"][:], R["eg"][:], ADD).then_inc(rt_d, 1)
        dve.wait_ge(rt_d, done.next())
        tt(R["esum"][:], R["esum"][:], R["gsum"][:], MUL).then_inc(rt_d, 1)
        dve.wait_ge(rt_d, done.next())
        dve.reciprocal(R["einv"][:], R["esum"][:]).then_inc(rt_d, 1)
        dve.wait_ge(rt_d, done.next())
        tt(R["wi"][:], R["ex"][:], R["einv"][:].unsqueeze(2).to_broadcast([P, 2, 8]), MUL).then_inc(rt_d, 1)
        dve.wait_ge(rt_d, done.next())
        for h in range(2):
            ins = tt(R["gates"][:, h], R["oh"][:, h].unsqueeze(2).to_broadcast([P, 4, 8]),
                     R["wi"][:, h].unsqueeze(1).to_broadcast([P, 4, 8]), MUL)
        ins.then_inc(rt_d, 1)
        dve.wait_ge(rt_d, done.next())
        assert done.n == 26, done.n
        dve.wait_ge(gt_done, 1)
        cp(R["gT"][:], wk[0:32, 1, 0:T]).then_inc(gT_ready, 1)
        dve.wait_ge(gT_ready, 1)

        base_m = BASE["moe"]
        with dve.Fori(0, ROUNDS) as r:
            with dve.Fori(0, 8) as e:
                n = r * 8 + e
                ts(R["rm"][:], R["gT"][:], ident[0:32, ds(n, 1)], MUL).then_inc(gb_rm, 1)
                dve.wait_ge(gb_done, n + 1)
                for c in range(2):
                    h = n * 6 + 3 * c
                    dve.wait_ge(evac_done, r * 48 + e * 4 + (base_m + 2 * c + 2))
                    dve.wait_ge(hid_split, n * 2 + c + 1)
                    tt(R["hid"][:], R["sa"][:, c, :], R["sb"][:, c, :], MUL).then_inc(vo_h, 1)
                    dve.wait_ge(vo_h, h + 1)
                    tt(R["hid"][:], R["hid"][:], wk[:, 0, 0:T], MUL).then_inc(vo_h, 1)
                    dve.wait_ge(vo_h, h + 2)
                    t = e * 2 + c
                    cp(dh[:, t, :], R["hid"][:]).then_inc(vo_h, 1)
                    dve.wait_ge(vo_h, h + 3)
                    tt(dl[:, t, :], R["hid"][:], dh[:, t, :].bitcast(F32), SUB).then_inc(hid_split, 1)
            with dve.Fori(0, 4) as c:
                for j in range(4):
                    k, q = slot(base_m + 32 + j)
                    add_out(k, r * 12 + c + q, c * 4 + j)
        dve.wait_ge(ot_used, 16 + ROUNDS * 16)
        rms(3, x)
        dve.wait_ge(rms_affine_done, 48)
        rms(4, x)
        split_lo(hb, 8)

        done = Count()
        dve.wait_ge(constC_in, 64)
        kv0 = BASE["kv"]
        KR, SQ, XR = C["kvraw"], C["kvsq"], C["xr"]
        dve.wait_ge(evac_done, kv0 + 4)
        dve.memset(XR[:], 0.0).then_inc(c0_d, 1)
        dve.wait_ge(c0_d, done.next())
        def blocks(kv):
            for a in range(2):
                for hd in range(2):
                    src = KR[:, 2 * kv + hd, 16 * a:16 * a + 240].rearrange("p (b c) -> p c b", c=16)
                    tt(XR[:, 16 * a:16 * a + 16, 16 * hd:16 * hd + 15], src,
                          C["pos"][:, kv, 16 * a:16 * a + 16].unsqueeze(2).to_broadcast([P, 16, 15]), ADD).then_inc(c0_d, 1)
                    dve.wait_ge(c0_d, done.next())
            hi, lo = (C["vrh"], C["vrl"]) if kv else (C["xrh"], C["xrl"])
            cp(hi[:], XR[:]).then_inc(c0_d, 1)
            dve.wait_ge(c0_d, done.next())
            tt(lo[:], XR[:], hi[:].bitcast(F32), SUB).then_inc(c0_d, 1)
            dve.wait_ge(c0_d, done.next())
        blocks(0)
        blocks(1)
        dve.wait_ge(evac_done, kv0 + 12)
        tt(SQ[:, 0:2, :], KR[:, 4:6, :], KR[:, 4:6, :], MUL).then_inc(c0_d, 1)
        dve.wait_ge(c0_d, done.next())
        tt(SQ[:, 2:4, :], KR[:, 8:10, :], KR[:, 8:10, :], MUL).then_inc(c0_d, 1)
        dve.wait_ge(c0_d, done.next())
        dve.wait_ge(c0_p, 1)
        ts(SQ[:].rearrange("p (a b) t -> p a (b t)", a=2), wk[:, 0:2, :], 1.0 / P, MUL, EPS, ADD).then_inc(c0_d, 1)
        dve.wait_ge(c0_d, done.next())
        dve.wait_ge(c0_a, 1)
        dve.reciprocal(SQ[:], SQ[:]).then_inc(c0_d, 1)
        dve.wait_ge(c0_d, done.next())
        stt(C["ks"][:, 0:2, :], KR[:, 4:6, :], vcol("nsa_k"), SQ[:, 0:2, :], MUL, MUL).then_inc(c0_d, 1)
        dve.wait_ge(c0_d, done.next())
        stt(C["ks"][:, 2:4, :], KR[:, 8:10, :], vcol("nsa_k"), SQ[:, 2:4, :], MUL, MUL).then_inc(c0_d, 1)
        dve.wait_ge(c0_d, done.next())

        dve.wait_ge(c0_p, 4)
        kc = C["kcn"][:].rearrange("p a b -> p (a b)")
        cp(kc, wk[:, 2, 0:32]).then_inc(c0_d, 1)
        dve.wait_ge(c0_d, done.next())
        tt(SQ[:, 0, 0:32], kc, kc, MUL).then_inc(c0_d, 1)
        dve.wait_ge(c0_d, done.next())
        dve.wait_ge(c0_p, 5)
        ts(SQ[:, 0, 0:32], wk[:, 0, 0:32], 1.0 / P, MUL, EPS, ADD).then_inc(c0_d, 1)
        dve.wait_ge(c0_d, done.next())
        dve.wait_ge(c0_a, 7)
        dve.reciprocal(SQ[:, 0, 0:32], SQ[:, 0, 0:32]).then_inc(c0_d, 1)
        dve.wait_ge(c0_d, done.next())
        stt(kc, kc, vcol("nsa_k"), SQ[:, 0, 0:32], MUL, MUL).then_inc(c0_d, 1)
        dve.wait_ge(c0_d, done.next())
        cp(C["vct"][:], wk[0:16, 3, 0:2 * P].rearrange("p (a b) -> p a b", a=2)).then_inc(c0_d, 1)
        dve.wait_ge(c0_d, done.next())
        dve.wait_ge(c0_a, 6)
        sp4 = C["sp4"]
        ts(sp4[:, 0:8], vec[:, VC["lru_lam"]:VC["lru_lam"] + 8], -1.0, MUL, 0.0, MAX).then_inc(c0_d, 1)
        dve.wait_ge(c0_d, done.next())
        tt(sp4[:, 0:8], sp4[:, 0:8], sp4[:, 8:16], ADD).then_inc(c0_d, 1)
        dve.wait_ge(c0_d, done.next())
        ts(sp4[:, 0:8], sp4[:, 0:8], 4.0, MUL).then_inc(c0_d, 1)
        dve.wait_ge(c0_d, done.next())
        dve.memset(C["raw"][:, 0:3], 0.0).then_inc(c0_d, 1)
        dve.wait_ge(c0_d, done.next())
        assert done.n == C0_D, done.n

        base_c = BASE["nsa"]

        def stage_c(g, s):
            if s is None:
                return
            done = Count(NC_D, s)

            dve.wait_ge(evac_done, base_c + 1 + s * 4)
            tt(C["qs"][:], C["q"][:], C["q"][:], MUL).then_inc(c_d, 1)
            dve.wait_ge(c_d, done.next())
            dve.wait_ge(evac_done, base_c + 4 + s * 4)
            dve.wait_ge(c_p, s * 5 + 1)
            ts(C["rq"][:], wk[:, 3, T:2 * T], 1.0 / P, MUL, EPS, ADD).then_inc(c_d, 1)
            dve.wait_ge(c_d, done.next())
            w = lambda tap: vcol("conv2", s * 4 + tap)
            ts(C["uc"][:], C["raw"][:, 0:T], w(0), MUL, vcol("conv2b", s), ADD).then_inc(c_d, 1)
            dve.wait_ge(c_d, done.next())
            for tap in range(1, 4):
                stt(C["uc"][:], C["raw"][:, tap:tap + T], w(tap), C["uc"][:], MUL, ADD).then_inc(c_d, 1)
                dve.wait_ge(c_d, done.next())
            tt(C["o"][:], C["ng"][:, 0, :], C["ng"][:, 1, :], MUL).then_inc(c_d, 1)
            dve.wait_ge(c_d, done.next())
            dve.wait_ge(c_a, s * NC_A + 1)
            dve.reciprocal(C["rq"][:], C["rq"][:]).then_inc(c_d, 1)
            dve.wait_ge(c_d, done.next())
            stt(C["qn"][:], C["q"][:], vcol("nsa_q"), C["rq"][:], MUL, MUL).then_inc(c_d, 1)
            dve.wait_ge(c_d, done.next())
            tt(C["qs"][:], C["lg"][:, 0, :], C["lg"][:, 1, :], MUL).then_inc(c_d, 1)
            dve.wait_ge(c_d, done.next())
            dve.wait_ge(c_p, s * 5 + 2)
            for i in range(2):
                ins = stt(C["z"][:, 2 * i:2 * i + 2, :], wk[:, i, :].rearrange("p (a t) -> p a t", a=2), SB_SCALE,
                          C["mask"][:], MUL, ADD)
            ins.then_inc(c_d, 1)
            dve.wait_ge(c_d, done.next())
            stt(C["zc"][:], wk[:, 3, T:T + 32].rearrange("p (a t) -> p a t", a=2), SB_SCALE, C["mcmp"][:], MUL, ADD).then_inc(c_d, 1)
            dve.wait_ge(c_d, done.next())
            red(C["mx"][:, 0:4], C["z"][:], MAX).then_inc(c_d, 1)
            dve.wait_ge(c_d, done.next())
            red(C["mx"][:, 4:6], C["zc"][:], MAX).then_inc(c_d, 1)
            dve.wait_ge(c_d, done.next())
            ts(C["mx"][:, 4:6], C["mx"][:, 4:6], NEG / 10, MAX).then_inc(c_d, 1)
            dve.wait_ge(c_d, done.next())
            ts(C["mx"][:, 0:6], C["mx"][:, 0:6], -1.0, MUL).then_inc(c_d, 1)
            dve.wait_ge(c_d, done.next())
            dve.wait_ge(c_a, s * NC_A + 7)
            ts(C["sm"][:, 0:6], C["sm"][:, 0:6], 1e-30, MAX).then_inc(c_d, 1)
            dve.wait_ge(c_d, done.next())
            dve.reciprocal(C["sm"][:, 0:6], C["sm"][:, 0:6]).then_inc(c_d, 1)
            dve.wait_ge(c_d, done.next())
            for i, (a, gi) in enumerate(((0, 1), (2, 2), (4, 0))):
                gate = C["gt"][:, :, ds(s * 3 + gi, 1)]
                o = C["sm"][:, a:a + 2].unsqueeze(2)
                tt(o, o, gate, MUL).then_inc(c_d, 1)
                dve.wait_ge(c_d, done.next())
            for j in range(4):
                ts(C["z"][:, j, :], C["z"][:, j, :], C["sm"][:, j:j + 1], MUL).then_inc(c_d, 1)
                dve.wait_ge(c_d, done.next())
            for j in range(2):
                ts(C["zc"][:, j, :], C["zc"][:, j, :], C["sm"][:, 4 + j:5 + j], MUL).then_inc(c_d, 1)
                dve.wait_ge(c_d, done.next())
            dve.wait_ge(c_a, s * NC_A + 10)
            ts(C["rcp"][:], C["th"][:], 1.0, ADD).then_inc(c_d, 1)
            dve.wait_ge(c_d, done.next())
            dve.reciprocal(C["rcp"][:], C["rcp"][:]).then_inc(c_d, 1)
            dve.wait_ge(c_d, done.next())
            ts(C["av"][:], C["th"][:], -1.0, MUL, 1.0, ADD).then_inc(c_d, 1)
            dve.wait_ge(c_d, done.next())
            tt(C["av"][:], C["av"][:], C["rcp"][:], MUL).then_inc(c_d, 1)
            dve.wait_ge(c_d, done.next())
            ts(C["th"][:], C["th"][:], 1e-30, MAX).then_inc(c_d, 1)
            dve.wait_ge(c_d, done.next())
            dve.wait_ge(c_a, s * NC_A + 13)
            stt(C["drv"][:], C["sqv"][:], 2.0, C["rcp"][:], MUL, MUL).then_inc(c_d, 1)
            dve.wait_ge(c_d, done.next())
            tt(C["drv"][:], C["drv"][:], C["ri"][:, 1, :], MUL).then_inc(c_d, 1)
            dve.wait_ge(c_d, done.next())
            tt(C["drv"][:], C["drv"][:], C["uc"][:], MUL).then_inc(c_d, 1)
            dve.wait_ge(c_d, done.next())
            dve.tensor_tensor_scan(C["hs"][:], C["av"][:], C["drv"][:], 0.0, MUL, ADD).then_inc(c_d, 1)
            dve.wait_ge(c_d, done.next())
            tt(C["hs"][:], C["hs"][:], C["qs"][:], MUL).then_inc(c_d, 1)
            dve.wait_ge(c_d, done.next())
            cp(yh[:, s, :], C["hs"][:]).then_inc(c_d, 1)
            dve.wait_ge(c_d, done.next())
            tt(yl[:, s, :], C["hs"][:], yh[:, s, :].bitcast(F32), SUB).then_inc(c_d, 1)
            dve.wait_ge(c_d, done.next())
            dve.wait_ge(c_p, s * 5 + 5)
            tt(C["o"][:], wk[:, 3, 0:T], C["o"][:], MUL).then_inc(c_d, 1)
            dve.wait_ge(c_d, done.next())
            cp(yh2[:, s, :], C["o"][:]).then_inc(c_d, 1)
            dve.wait_ge(c_d, done.next())
            tt(yl2[:, s, :], C["o"][:], yh2[:, s, :].bitcast(F32), SUB).then_inc(c_d, 1)
            dve.wait_ge(c_d, done.next())
            done.check()

        heads(dve, stage_c)
        merge_g("g_a", G["sg"], ptmp2, True)
        merge_g("g_b", G["sg"], ptmp2)

        done = Count()
        dve.wait_ge(rowf_a, 3)
        stt(E["f"][:], foxf[0:8, :], 0.0, E["l"][:], MIN, SUB).then_inc(rowf_d, 1)
        dve.wait_ge(rowf_d, done.next())
        dve.tensor_tensor_scan(E["c"][:], one_row(8), E["f"][:], 0.0, MUL, ADD).then_inc(rowf_d, 1)
        dve.wait_ge(rowf_d, done.next())
        dve.wait_ge(rowf_t, 1)
        cp(E["ccol"][:], wk[:, 0, 0:16].rearrange("p (a b) -> p a b", a=2)).then_inc(rowf_d, 1)
        dve.wait_ge(rowf_d, done.next())
        dve.wait_ge(constE_in, 16)
        base_d = BASE["fox"]

        def stage_d(g, s):
            if s is None:
                return
            done = Count(ND_D, s)

            ts(E["rm"][:], E["c"][:], ident[0:8, ds(s, 1)], MUL, -1.0, MUL).then_inc(d_d, 1)
            dve.wait_ge(d_d, done.next())
            dve.wait_ge(evac_done, base_d + 2 + s * 4)
            tt(E["qks"][:], E["qk"][:], E["qk"][:], MUL).then_inc(d_d, 1)
            dve.wait_ge(d_d, done.next())
            dve.wait_ge(d_p, s * 5 + 1)
            ts(E["rqk"][:], wk[:, 1, :].rearrange("p (a t) -> p a t", a=2), 1.0 / P, MUL, EPS, ADD).then_inc(d_d, 1)
            dve.wait_ge(d_d, done.next())
            dve.wait_ge(d_p, s * 5 + 2)
            for j in range(2):
                stt(E["cb"][:, j, :], wk[:, 2, 0:T], E["ccol"][:, j, ds(s, 1)], E["mask"][:, j, :], ADD, ADD).then_inc(d_d, 1)
                dve.wait_ge(d_d, done.next())
            dve.wait_ge(evac_done, base_d + 4 + s * 4)
            tt(E["o"][:], E["fg"][:, 0, :], E["fg"][:, 1, :], MUL).then_inc(d_d, 1)
            dve.wait_ge(d_d, done.next())
            dve.wait_ge(d_a, s * ND_A + 1)
            dve.reciprocal(E["rqk"][:], E["rqk"][:]).then_inc(d_d, 1)
            dve.wait_ge(d_d, done.next())
            stt(E["qk"][:, 0, :], E["qk"][:, 0, :], vcol("fox_q"), E["rqk"][:, 0, :], MUL, MUL).then_inc(d_d, 1)
            dve.wait_ge(d_d, done.next())
            stt(E["qk"][:, 1, :], E["qk"][:, 1, :], vcol("fox_k"), E["rqk"][:, 1, :], MUL, MUL).then_inc(d_d, 1)
            dve.wait_ge(d_d, done.next())
            dve.wait_ge(d_p, s * 5 + 3)
            stt(E["z"][:], wk[:, 0, :].rearrange("p (a t) -> p a t", a=2), SB_SCALE, E["cb"][:], MUL, ADD).then_inc(d_d, 1)
            dve.wait_ge(d_d, done.next())
            red(E["mx"][:], E["z"][:], MAX).then_inc(d_d, 1)
            dve.wait_ge(d_d, done.next())
            ts(E["mx"][:], E["mx"][:], -1.0, MUL).then_inc(d_d, 1)
            dve.wait_ge(d_d, done.next())
            dve.wait_ge(d_a, s * ND_A + 4)
            ts(E["sm"][:], E["sm"][:], 1e-30, MAX).then_inc(d_d, 1)
            dve.wait_ge(d_d, done.next())
            dve.reciprocal(E["sm"][:], E["sm"][:]).then_inc(d_d, 1)
            dve.wait_ge(d_d, done.next())
            for j in range(2):
                ts(E["z"][:, j, :], E["z"][:, j, :], E["sm"][:, j:j + 1], MUL).then_inc(d_d, 1)
                dve.wait_ge(d_d, done.next())
            dve.wait_ge(d_p, s * 5 + 5)
            tt(E["o"][:], wk[:, 3, 0:T], E["o"][:], MUL).then_inc(d_d, 1)
            dve.wait_ge(d_d, done.next())
            cp(yh[:, s, :], E["o"][:]).then_inc(d_d, 1)
            dve.wait_ge(d_d, done.next())
            tt(yl[:, s, :], E["o"][:], yh[:, s, :].bitcast(F32), SUB).then_inc(d_d, 1)
            dve.wait_ge(d_d, done.next())
            done.check()

        heads(dve, stage_d)
        merge_g("g_c", G["sg"], ptmp2)

        split_merged(2)
        dve.wait_ge(gelu_done, 4)
        tt(G["pl"][:], G["po"][:], G["ph"][:].bitcast(F32), SUB).then_inc(y_split, 1)
        each(dve, BASE["wout2"], 16, lambda k, q, t: add_out(k, q, t, G["sg"]))
        dve.wait_ge(ot_used, 16 + ROUNDS * 16 + 16)
        split_lo(x, 12)
        dve.wait_ge(evac_done, BASE["ple"] + 2)
        rms(5, merged)
        dve.wait_ge(rms_affine_done, 64 + 16)

        def last(k, q, t):
            n = q * 4 + k
            dve.wait_ge(evac_done, n + 1)
            tt(G["sg"][:, k % 2, :], G["sg"][:, k % 2, :], merged[:, t, :], MUL).then_inc(vo_l, 1)
            dve.wait_ge(vo_l, t + 1)
            tt(x[:, t, :], x[:, t, :], G["sg"][:, k % 2, :], ADD).then_inc(ot_used, 1)
        each(dve, BASE["pgate"], 16, last)

    block_cm.__exit__(None, None, None)


def _tiles(w, kt):
    k, c = w.shape
    per = 16 // kt
    t = w.reshape(k // (kt * P), kt, P, c // P, P)
    t = t.reshape(k // (kt * P), kt, P, c // P // per, per, P).transpose(3, 0, 2, 4, 1, 5)
    return t.reshape(-1, P, CH)


def _cols(v):
    return v.reshape(-1, P).T


def _layout(i):
    import numpy as np

    f = np.float32
    main = np.empty((NMAIN, P, CH), f)
    a = {}

    def put(name, w, kt=DT, at=0):
        t = _tiles(w, kt)
        main[BASE[name] + at:BASE[name] + at + len(t)] = t

    def padded(w, parts):
        o = np.zeros((w.shape[0], P), f)
        for to, frm, n in parts:
            o[:, to:to + n] = w[:, frm:frm + n]
        return o

    def interleave(w, groups, n):
        return np.concatenate([w[..., c + h * s:c + (h + 1) * s] for h in range(n) for c, s in groups], axis=-1)

    w = i["w_in"][0]
    put("sb", interleave(w, [(0, P), (1024, P), (2048, P), (3072, P)], 8))
    put("ml", interleave(w, [(4096, 256), (5120, 256), (6144, 256), (7168, 256)], 4))
    put("mlif", padded(w, [(0, 8192, 4), (32, 8196, 4)]))
    ada = i["w_ada"][0].reshape(DT, P, 6, CH).transpose(2, 0, 1, 3)
    for v, name, c in ((3, "g_sb", 8200), (4, "g_s5", 10248), (5, "g_ml", 12296)):
        t = _tiles(w[:, c:c + D], DT)
        m = main[BASE[name]:BASE[name] + 32].reshape(8, 2, 2, P, CH)
        m[:, 0] = t.reshape(8, 2, P, CH)
        m[:, 1] = ada[v].reshape(8, 2, P, CH)
    for name in ("p_sb", "p_s5", "p_ml"):
        put(name, i[name][0], WT)
    put("glu", i["s5_w_glu"][0], WT)
    put("wout", i["w_out"][0])
    rt = np.zeros((D, P), f)
    rt[:, 0:4] = i["moe_w_group"][0]
    rt[:, 32:64] = i["moe_w_router"][0]
    put("router", rt)
    w1, w3, w2 = i["moe_w1"][0], i["moe_w3"][0], i["moe_w2"][0]
    for e in range(N_EXP):
        at = e // 8 * 48 + e % 8 * 4
        t1, t3 = _tiles(w1[e], DT), _tiles(w3[e], DT)
        for c in range(2):
            main[BASE["moe"] + at + 2 * c] = t1[c]
            main[BASE["moe"] + at + 2 * c + 1] = t3[c]
    for r in range(ROUNDS):
        put("moe", w2[8 * r:8 * r + 8].reshape(D, D), at=r * 48 + 32)
    w = i["w_in_2"][0]
    b = i["b_in_2"][0]
    groups_nsa = [(2048, P), (4632, P), (0, P), (1024, P)]
    groups_fox = [(5656, P), (6680, P), (7704, P), (8736, P)]
    put("kv", w[:, 3072:4608])
    put("bf", padded(w, [(0, 4608, 24), (32, 8728, 8)]))
    put("nsa", interleave(w, groups_nsa, 8))
    put("fox", interleave(w, groups_fox, 8))
    for n, name in enumerate(("g_a", "g_b", "g_c")):
        put(name, w[:, 9760 + n * D:9760 + (n + 1) * D])
    for n, name in enumerate(("p_a", "p_b", "p_c")):
        put(name, i["w_branch_2"][0, n], WT)
    for kv in range(2):
        at = BASE["cmp"] + 4 * kv
        main[at:at + 4] = i["cmp_w1_2"][0, kv].reshape(4, 8, P, T).transpose(0, 2, 1, 3).reshape(4, P, CH)
    put("wout2", i["w_out_2"][0])
    put("ple", i["w_ple_2"][0], 2)
    put("pgate", i["w_ple_gate_2"][0])
    a["main"] = main
    a["ada"] = np.ascontiguousarray(ada[0:3]).reshape(NADA, P, CH)

    vec = np.zeros((P, NV), f)

    def v(name, val, rows=slice(None)):
        val = np.asarray(val)
        vec[rows, VC[name]:VC[name] + val.shape[1]] = val
    v("b_ada", _cols(i["b_ada"][0]))
    for name, src in (("g_mix", "norm_mix_g"), ("g_moe", "norm_moe_g"), ("g_ln2", "ln_gain_2"), ("g_ple", "ple_gain_2"),
                      ("conv2b", "conv_b_2"), ("lru_ba", "lru_ba_2"), ("lru_bx", "lru_bx_2"), ("lru_lam", "lru_lambda_2"),
                      ("s5_d", "s5_d"), ("nsa_q", "nsa_q_gain_2"), ("nsa_k", "nsa_k_gain_2"), ("fox_q", "fox_q_gain_2"),
                      ("fox_k", "fox_k_gain_2")):
        v(name, _cols(i[src][0]))
    v("g_fin", _cols(i["final_g"]))
    v("c", _cols(i["c"][0]))
    b2 = np.concatenate([b[3072:4608], padded(b[None], [(0, 4608, 24), (32, 8728, 8)])[0], interleave(b, groups_nsa, 8),
                         b[9760:9760 + 2 * D], interleave(b, groups_fox, 8), b[9760 + 2 * D:9760 + 3 * D]])
    v("b2", _cols(b2))
    v("conv2", i["conv_w_2"][0].reshape(4, 8, P).transpose(2, 1, 0).reshape(P, 32))
    cw = i["ml_conv"][0].reshape(4, 2, 4, 2, P)
    v("conv", cw.transpose(4, 2, 1, 3, 0).reshape(P, 64))
    v("b_if", i["ml_i_bias"][0][:, None], slice(0, 4))
    v("b_if", i["ml_f_bias"][0][:, None], slice(32, 36))
    v("b_rt", i["moe_b_group"][0][:, None], slice(0, 4))
    v("b_rt", i["moe_b_router"][0][:, None], slice(32, 64))
    v("quarter", np.full((P, 1), TWO_PI / 4, f))
    v("one", np.ones((P, 1), f))
    pairs = lambda m: m.reshape(32, 2, 64).transpose(1, 2, 0).reshape(P, 32)
    v("lam_re", pairs(i["s5_lam_re"][0]))
    v("lam_im", pairs(i["s5_lam_im"][0]))
    v("log_dt", pairs(np.repeat(i["s5_log_dt"][0][:, None], 64, 1)))
    a["vec"] = vec

    s5b = np.zeros((8, 4, 2, 16, 2, 2, 64), f)
    s5c = np.zeros((8, 2, 64, 4, 2, 2, 16), f)
    for c, part in enumerate(("re", "im")):
        bm = i["s5_b_" + part][0].reshape(8, 4, 2, 64, 16)
        cm = i["s5_c_" + part][0].reshape(8, 4, 2, 16, 64)
        for g in range(2):
            s5b[:, :, g, :, c, g, :] = bm[:, :, g].transpose(0, 1, 3, 2)
            s5c[:, g, :, :, c, g, :] = cm[:, :, g].transpose(0, 3, 1, 2)
    a["s5_b"] = s5b.reshape(8, P, 2, P)
    a["s5_c"] = s5c.reshape(8, P, 4, 2, 32)
    lw = np.zeros((8, 2, 64, 2, 2, 64), f)
    for m, name in enumerate(("lru_wa_2", "lru_wx_2")):
        lm = i[name][0].reshape(8, 2, 64, 64)
        for g in range(2):
            lw[:, g, :, m, g, :] = lm[:, g]
    a["lru_w"] = lw.reshape(8, P, 2, P)
    a["pos"] = np.ascontiguousarray(i["cmp_pos_2"][0].transpose(2, 0, 1))
    a["cmp_w2"] = np.ascontiguousarray(i["cmp_w2_2"][0].reshape(4, P, P).transpose(1, 0, 2))
    chan = lambda m, n: np.ascontiguousarray(m.T.reshape(n, P, T).transpose(1, 0, 2))
    a["x"] = chan(i["x"][0], DT)
    a["p"] = chan(i["p_2"][0, 0], 2)

    r = np.arange(P)
    key = (np.arange(2)[None, :] * P + r[:, None])[:, :, None]
    tok = np.arange(T)[None, None, :]
    a["ident"] = np.eye(P, dtype=f)
    a["ones"] = np.ones((P, P), f)
    a["tri"] = (r[:, None] >= r[None, :]).astype(f)
    a["iota"] = np.tile(np.arange(T, dtype=f), (P, 1))
    a["mask_strict"] = (key < tok).astype(f)
    a["mask_incl"] = (key <= tok).astype(f)
    a["mask_neg"] = np.where(tok <= key, 0, NEG).astype(f)
    blk = np.arange(16)[None, None, :]
    a["mask_cmp"] = np.where((blk < N_CMP) & (16 * blk + 31 <= key), 0, NEG).astype(f)
    lower = lambda n: (np.arange(n)[None, :] < np.arange(n)[:, None]).astype(f).ravel()
    a["tri_small"] = np.tile(np.concatenate([lower(8), lower(4)]), (P, 1))
    return a


def kernel(**inputs):
    import numpy as np
    import concourse.bacc as bacc
    from concourse.bass_utils import run_bass_kernel_spmd as run

    arrays = _layout({k: np.asarray(v) for k, v in inputs.items()})
    nc = bacc.Bacc("TRN2", target_bir_lowering=False, num_devices=1)
    dr = {k: nc.dram_tensor("in_" + k, v.shape, F32, kind="ExternalInput").ap() for k, v in arrays.items()}
    dr["out"] = nc.dram_tensor("out_0", (P, DT, T), F32, kind="ExternalOutput").ap()
    build(nc, dr)
    r = run(nc, [{"in_" + k: v for k, v in arrays.items()}], core_ids=[0])
    out = r.results[0]["out_0"]
    return np.ascontiguousarray(out.transpose(2, 1, 0).reshape(1, T, D))
```
